# Optimizing a Trainium2 kernel written in Bass

```python
import math
import jax, jax.numpy as jnp
from jax import lax
import numpy as np

D_MODEL = 1024
BATCH = 1
SEQ = 256
DEPTH = 2

GRID_W = 64
CTX_LEN = 256
N_EVEN = (DEPTH + 1) // 2
N_ODD = DEPTH // 2
EPS = 1e-6

ROPE_HEAD_DIM = 64
ROPE_FREQS = ROPE_HEAD_DIM // 4
ROPE_BASE = 10000.0

SC_WIDTH = D_MODEL // 2
DA_HEADS = 4
DA_HEAD_DIM = ROPE_HEAD_DIM
DA_V_DIM = 2 * DA_HEAD_DIM
DA_QK_WIDTH = DA_HEADS * 2 * DA_HEAD_DIM
DA_WIDTH = DA_HEADS * DA_V_DIM
Q_BLOCK = 128
EVEN_SPLITS = (SC_WIDTH, 2 * SC_WIDTH, 3 * SC_WIDTH, 3 * SC_WIDTH + DA_QK_WIDTH, 3 * SC_WIDTH + 2 * DA_QK_WIDTH)
EVEN_IN = 3 * SC_WIDTH + 2 * DA_QK_WIDTH + DA_WIDTH
EVEN_OUT = SC_WIDTH + DA_WIDTH

POOL_WINDOWS = (2, 4, 8, 16)
POOL_RADII = tuple(w // 2 for w in POOL_WINDOWS)
POOL_GROUPS = 4
POOL_WIDTH = D_MODEL // 2
POOL_GROUP_DIM = POOL_WIDTH // POOL_GROUPS
RET_HEADS = 4
RET_QK_DIM = ROPE_HEAD_DIM
RET_V_DIM = 2 * RET_QK_DIM
RET_QK_WIDTH = RET_HEADS * RET_QK_DIM
RET_WIDTH = RET_HEADS * RET_V_DIM
RET_CHUNK = 128
ODD_SPLITS = (POOL_WIDTH, POOL_WIDTH + RET_QK_WIDTH, POOL_WIDTH + 2 * RET_QK_WIDTH, POOL_WIDTH + 2 * RET_QK_WIDTH + RET_WIDTH)
ODD_IN = POOL_WIDTH + 2 * RET_QK_WIDTH + 2 * RET_WIDTH
ODD_OUT = POOL_WIDTH + RET_WIDTH

FFN_DIM = 2816


def rms_norm(x, g):
    xf = x.astype(jnp.float32)
    y = xf * lax.rsqrt(jnp.mean(xf * xf, axis=-1, keepdims=True) + EPS)
    return (y * g.astype(jnp.float32)).astype(x.dtype)

def modulate(h, shift, scale):
    return h * (1 + scale) + shift

def dwconv3(x, w):
    xp = jnp.pad(x, ((0, 0), (1, 1), (0, 0)))
    return xp[:, :-2] * w[0] + xp[:, 1:-1] * w[1] + xp[:, 2:] * w[2]

def rope_tables(rows):
    row = jnp.repeat(jnp.arange(rows, dtype=jnp.float32), GRID_W)
    col = jnp.tile(jnp.arange(GRID_W, dtype=jnp.float32), rows)
    inv = ROPE_BASE ** (-jnp.arange(ROPE_FREQS, dtype=jnp.float32) / ROPE_FREQS)
    ang = jnp.stack([row[:, None] * inv, col[:, None] * inv], axis=1)
    return jnp.cos(ang), jnp.sin(ang)

def apply_rope(x, cos, sin):
    shp = x.shape
    xr = x.reshape(*shp[:-1], 2, 2, ROPE_FREQS)
    bc = (shp[1],) + (1,) * (x.ndim - 3) + (2, ROPE_FREQS)
    c = cos.reshape(bc).astype(x.dtype)
    s = sin.reshape(bc).astype(x.dtype)
    x1, x2 = xr[..., 0, :], xr[..., 1, :]
    out = jnp.stack([x1 * c - x2 * s, x1 * s + x2 * c], axis=-2)
    return out.reshape(shp)

def conv_ffn(h, w_up, conv_w, conv_b, w_down):
    a, b = jnp.split(h @ w_up, 2, axis=-1)
    a = dwconv3(a, conv_w) + conv_b
    return (jax.nn.silu(a) * b) @ w_down

def diff_lambda_init(layer_idx):
    return 0.8 - 0.6 * math.exp(-0.3 * layer_idx)

def diff_attend(q, k, v, lam):
    s = jnp.einsum('bhmqd,bhmkd->bhmqk', q, k).astype(jnp.float32) * (DA_HEAD_DIM ** -0.5)
    p = jax.nn.softmax(s, axis=-1)
    p = p[:, :, 0] - lam * p[:, :, 1]
    return jnp.einsum('bhqk,bhkv->bhqv', p.astype(v.dtype), v)

def conv_diff_mixer(h_ctx, h_lat, w_in, w_out, sc_conv_w, q_g, k_g, lq1, lk1, lq2, lk2, subln_g, lam_init, cos, sin):
    f32 = jnp.float32
    lam = (jnp.exp(jnp.sum(lq1.astype(f32) * lk1.astype(f32)))
           - jnp.exp(jnp.sum(lq2.astype(f32) * lk2.astype(f32))) + lam_init)

    def project(h, rotate):
        b_g, c_g, xv, q, k, v = jnp.split(h @ w_in, EVEN_SPLITS, axis=-1)
        B_, N = h.shape[:2]
        q = rms_norm(q.reshape(B_, N, DA_HEADS, 2, DA_HEAD_DIM), q_g)
        k = rms_norm(k.reshape(B_, N, DA_HEADS, 2, DA_HEAD_DIM), k_g)
        if rotate:
            q = apply_rope(q, cos, sin)
            k = apply_rope(k, cos, sin)
        q = q.transpose(0, 2, 3, 1, 4)
        k = k.transpose(0, 2, 3, 1, 4)
        v = v.reshape(B_, N, DA_HEADS, DA_V_DIM).transpose(0, 2, 1, 3)
        return (b_g, c_g, xv), q, k, v

    def finish(gates, o):
        b_g, c_g, xv = gates
        y_conv = b_g * dwconv3(c_g * xv, sc_conv_w)
        B_, _, N, _ = o.shape
        o = rms_norm(o.transpose(0, 2, 1, 3), subln_g) * (1.0 - lam_init)
        return jnp.concatenate([y_conv, o.reshape(B_, N, DA_WIDTH).astype(y_conv.dtype)], axis=-1) @ w_out

    gates_c, qc, kc, vc = project(h_ctx, False)
    gates_l, ql, kl, vl = project(h_lat, True)
    k_all = jnp.concatenate([kl, kc], axis=3)
    v_all = jnp.concatenate([vl, vc], axis=2)
    B_, H, _, N, d = ql.shape
    nb = N // Q_BLOCK
    q_blocks = jnp.moveaxis(ql.reshape(B_, H, 2, nb, Q_BLOCK, d), 3, 0)
    o_blocks = lax.map(lambda qb: diff_attend(qb, k_all, v_all, lam), q_blocks)
    o_lat = jnp.moveaxis(o_blocks, 0, 2).reshape(B_, H, N, DA_V_DIM)
    y_lat = finish(gates_l, o_lat)
    y_ctx = finish(gates_c, diff_attend(qc, kc, vc, lam))
    return y_ctx, y_lat

def multiscale_pool(v, pool_w, pool_scale):
    B_, N, _ = v.shape
    vg = v.reshape(B_, N, POOL_GROUPS, POOL_GROUP_DIM).astype(jnp.float32)
    cs = jnp.concatenate([jnp.zeros_like(vg[:, :1]), jnp.cumsum(vg, axis=1)], axis=1)
    t = jnp.arange(N)[:, None]
    r = jnp.array(POOL_RADII)[None, :]
    lo = jnp.clip(t - r, 0, N)
    hi = jnp.clip(t + r + 1, 0, N)
    g = jnp.arange(POOL_GROUPS)[None, :]
    mean = (cs[:, hi, g] - cs[:, lo, g]) / (hi - lo).astype(jnp.float32)[:, :, None]
    y = (mean - vg).astype(v.dtype)
    y = jnp.einsum('bngc,gcd->bngd', y, pool_w)
    return y.reshape(B_, N, POOL_WIDTH) * pool_scale

def retention_scan(q, k, v, lg, s0):
    B_, H, N, _ = q.shape
    dv = v.shape[-1]
    nc = N // RET_CHUNK

    def chunks(t):
        return jnp.moveaxis(t.reshape(B_, H, nc, RET_CHUNK, t.shape[-1]), 2, 0)

    pos = jnp.arange(RET_CHUNK, dtype=jnp.float32)
    diff = pos[:, None] - pos[None, :]
    intra = jnp.where(diff >= 0, jnp.exp(lg[:, None, None] * jnp.maximum(diff, 0.0)), 0.0)
    q_dec = jnp.exp(lg[:, None] * (pos + 1.0))[None, :, :, None]
    k_dec = jnp.exp(lg[:, None] * (RET_CHUNK - 1.0 - pos))[None, :, :, None]
    c_dec = jnp.exp(lg * RET_CHUNK)[None, :, None, None]

    def step(s, qkv):
        qc, kc, vc = qkv
        att = jnp.einsum('bhid,bhjd->bhij', qc, kc) * intra
        o = jnp.einsum('bhij,bhjv->bhiv', att, vc) + jnp.einsum('bhid,bhdv->bhiv', qc * q_dec, s)
        s = s * c_dec + jnp.einsum('bhjd,bhjv->bhdv', kc * k_dec, vc)
        return s, o

    _, o = lax.scan(step, s0, (chunks(q), chunks(k), chunks(v)))
    return jnp.moveaxis(o, 0, 2).reshape(B_, H, N, dv)

def retention_bidir(q, k, v, lg_f, lg_b, s_f, s_b):
    o_f = retention_scan(q, k, v, lg_f, s_f)
    flip = lambda t: jnp.flip(t, axis=2)
    o_b = flip(retention_scan(flip(q), flip(k), flip(v), lg_b, s_b))
    return o_f + o_b

def context_states(k, v, lg_f, lg_b):
    L = k.shape[2]
    j = jnp.arange(L, dtype=jnp.float32)
    w_f = jnp.exp(lg_f[:, None] * (L - 1.0 - j))
    w_b = jnp.exp(lg_b[:, None] * j)
    s_f = jnp.einsum('bhjd,hj,bhjv->bhdv', k, w_f, v)
    s_b = jnp.einsum('bhjd,hj,bhjv->bhdv', k, w_b, v)
    return s_f, s_b

def pool_retention_mixer(h_ctx, h_lat, w_in, w_out, pool_w, pool_scale, dec_f, dec_b, gn_g, cos, sin, with_ctx):
    f32 = jnp.float32
    lg_f = -jnp.exp(dec_f.astype(f32))
    lg_b = -jnp.exp(dec_b.astype(f32))

    def heads(t, dh):
        B_, N = t.shape[:2]
        return t.reshape(B_, N, RET_HEADS, dh)

    def qkv_heads(q, k, v, rotate):
        q, k, v = heads(q, RET_QK_DIM), heads(k, RET_QK_DIM), heads(v, RET_V_DIM)
        if rotate:
            q = apply_rope(q, cos, sin)
            k = apply_rope(k, cos, sin)
        q = (q.astype(f32) * (RET_QK_DIM ** -0.5)).transpose(0, 2, 1, 3)
        k = k.astype(f32).transpose(0, 2, 1, 3)
        v = v.astype(f32).transpose(0, 2, 1, 3)
        return q, k, v

    def finish(pv, g, o):
        B_, _, N, _ = o.shape
        y_r = rms_norm(o.transpose(0, 2, 1, 3), gn_g).reshape(B_, N, RET_WIDTH).astype(g.dtype) * jax.nn.silu(g)
        y_p = multiscale_pool(pv, pool_w, pool_scale)
        return jnp.concatenate([y_p, y_r], axis=-1) @ w_out

    pv_l, q_l, k_l, v_l, g_l = jnp.split(h_lat @ w_in, ODD_SPLITS, axis=-1)
    ql, kl, vl = qkv_heads(q_l, k_l, v_l, True)
    if with_ctx:
        pv_c, q_c, k_c, v_c, g_c = jnp.split(h_ctx @ w_in, ODD_SPLITS, axis=-1)
        qc, kc, vc = qkv_heads(q_c, k_c, v_c, False)
    else:
        k_c, v_c = jnp.split(h_ctx @ w_in[:, ODD_SPLITS[1]:ODD_SPLITS[3]], [RET_QK_WIDTH], axis=-1)
        kc = heads(k_c, RET_QK_DIM).astype(f32).transpose(0, 2, 1, 3)
        vc = heads(v_c, RET_V_DIM).astype(f32).transpose(0, 2, 1, 3)
    s_f, s_b = context_states(kc, vc, lg_f, lg_b)
    y_lat = finish(pv_l, g_l, retention_bidir(ql, kl, vl, lg_f, lg_b, s_f, s_b))
    y_ctx = None
    if with_ctx:
        zero = jnp.zeros_like(s_f)
        y_ctx = finish(pv_c, g_c, retention_bidir(qc, kc, vc, lg_f, lg_b, zero, zero))
    return y_ctx, y_lat

def first_inputs(seed: int = 0) -> dict:
    key = jax.random.key(seed)
    ks = iter(jax.random.split(key, 40))

    def nrm(shape, scale=1.0):
        return scale * jax.random.normal(next(ks), shape, jnp.float32)

    def gain(shape):
        return 1.0 + nrm(shape, 0.05)

    base_decay = jnp.log(-jnp.log1p(-(2.0 ** (-5.0 - jnp.arange(RET_HEADS, dtype=jnp.float32)))))
    return {
        'x': nrm((BATCH, SEQ, D_MODEL)),
        'c': nrm((BATCH, D_MODEL)),
        'ctx': nrm((BATCH, CTX_LEN, D_MODEL)),
        'c_ctx': nrm((D_MODEL,)),
        'mod_w': nrm((DEPTH, D_MODEL, 6 * D_MODEL), 0.5 * D_MODEL ** -0.5),
        'mod_b': nrm((DEPTH, 6 * D_MODEL), 0.01),
        'norm1_g': gain((DEPTH, D_MODEL)),
        'norm2_g': gain((DEPTH, D_MODEL)),
        'ev_w_in': nrm((N_EVEN, D_MODEL, EVEN_IN), D_MODEL ** -0.5),
        'ev_w_out': nrm((N_EVEN, EVEN_OUT, D_MODEL), EVEN_OUT ** -0.5),
        'sc_conv_w': nrm((N_EVEN, 3, SC_WIDTH), 3 ** -0.5),
        'da_q_norm': gain((N_EVEN, DA_HEAD_DIM)),
        'da_k_norm': gain((N_EVEN, DA_HEAD_DIM)),
        'da_lq1': nrm((N_EVEN, DA_HEAD_DIM), 0.1),
        'da_lk1': nrm((N_EVEN, DA_HEAD_DIM), 0.1),
        'da_lq2': nrm((N_EVEN, DA_HEAD_DIM), 0.1),
        'da_lk2': nrm((N_EVEN, DA_HEAD_DIM), 0.1),
        'da_subln_g': gain((N_EVEN, DA_V_DIM)),
        'od_w_in': nrm((N_ODD, D_MODEL, ODD_IN), D_MODEL ** -0.5),
        'od_w_out': nrm((N_ODD, ODD_OUT, D_MODEL), ODD_OUT ** -0.5),
        'pool_w': nrm((N_ODD, POOL_GROUPS, POOL_GROUP_DIM, POOL_GROUP_DIM), POOL_GROUP_DIM ** -0.5),
        'pool_scale': gain((N_ODD, POOL_WIDTH)),
        'ret_decay_f': base_decay + nrm((N_ODD, RET_HEADS), 0.1),
        'ret_decay_b': base_decay + nrm((N_ODD, RET_HEADS), 0.1),
        'ret_gn_g': gain((N_ODD, RET_V_DIM)),
        'ffn_w_up': nrm((DEPTH, D_MODEL, 2 * FFN_DIM), D_MODEL ** -0.5),
        'ffn_conv_w': nrm((DEPTH, 3, FFN_DIM), 3 ** -0.5),
        'ffn_conv_b': nrm((DEPTH, FFN_DIM), 0.01),
        'ffn_w_down': nrm((DEPTH, FFN_DIM, D_MODEL), FFN_DIM ** -0.5),
    }

def first_block(x, c, ctx, c_ctx, mod_w, mod_b, norm1_g, norm2_g, ev_w_in, ev_w_out, sc_conv_w, da_q_norm, da_k_norm,
              da_lq1, da_lk1, da_lq2, da_lk2, da_subln_g, od_w_in, od_w_out, pool_w, pool_scale, ret_decay_f,
              ret_decay_b, ret_gn_g, ffn_w_up, ffn_conv_w, ffn_conv_b, ffn_w_down):
    ROWS = x.shape[1] // GRID_W
    cos, sin = rope_tables(ROWS)
    silu_c = jax.nn.silu(c)
    silu_cc = jax.nn.silu(c_ctx)
    for i in range(DEPTH):
        last = i == DEPTH - 1
        j = i // 2
        mod_l = (silu_c @ mod_w[i] + mod_b[i])[:, None, :]
        mod_c = silu_cc @ mod_w[i] + mod_b[i]
        sh1, sc1, g1, sh2, sc2, g2 = jnp.split(mod_l, 6, axis=-1)
        sh1c, sc1c, g1c, sh2c, sc2c, g2c = jnp.split(mod_c, 6, axis=-1)
        h_lat = modulate(rms_norm(x, norm1_g[i]), sh1, sc1)
        h_ctx = modulate(rms_norm(ctx, norm1_g[i]), sh1c, sc1c)
        if i % 2 == 0:
            y_ctx, y_lat = conv_diff_mixer(h_ctx, h_lat, ev_w_in[j], ev_w_out[j], sc_conv_w[j], da_q_norm[j],
                                           da_k_norm[j], da_lq1[j], da_lk1[j], da_lq2[j], da_lk2[j],
                                           da_subln_g[j], diff_lambda_init(i), cos, sin)
        else:
            y_ctx, y_lat = pool_retention_mixer(h_ctx, h_lat, od_w_in[j], od_w_out[j], pool_w[j], pool_scale[j],
                                                ret_decay_f[j], ret_decay_b[j], ret_gn_g[j], cos, sin, not last)
        x = x + g1 * y_lat
        x = x + g2 * conv_ffn(modulate(rms_norm(x, norm2_g[i]), sh2, sc2),
                              ffn_w_up[i], ffn_conv_w[i], ffn_conv_b[i], ffn_w_down[i])
        if not last:
            ctx = ctx + g1c * y_ctx
            ctx = ctx + g2c * conv_ffn(modulate(rms_norm(ctx, norm2_g[i]), sh2c, sc2c),
                                       ffn_w_up[i], ffn_conv_w[i], ffn_conv_b[i], ffn_w_down[i])
    return x


DEPTH_2 = 1

D_ATTN = D_MODEL // 2
HEAD_DIM_A = 64
N_HEADS_A = D_ATTN // HEAD_DIM_A
DILATED_PAIRS = ((128, 1), (512, 4), (2048, 16))
D_REC = D_MODEL - D_ATTN
HGRN_EXPAND = 128
N_HEADS_R = D_REC // HGRN_EXPAND
HEAD_DIM_R = D_REC // N_HEADS_R
HGRN_CHUNK = 32
D_FORGET = N_HEADS_R * HGRN_EXPAND
D_IN = 3 * D_ATTN + 2 * D_FORGET + 2 * D_REC
N_EXPERTS = 32
TOP_K = 4
D_FF = D_MODEL
SWIGLU_LIMIT = 7.0
SWIGLU_ALPHA = 1.702
MOE_BLOCK = 128


def rms_norm_2(x, w):
    xf = x.astype(jnp.float32)
    y = xf * lax.rsqrt(jnp.mean(xf * xf, axis=-1, keepdims=True) + EPS)
    return (y * w.astype(jnp.float32)).astype(x.dtype)

def modulate_2(n, shift, scale):
    return n * (1.0 + scale[:, None, :]) + shift[:, None, :]

def dilated_causal_attention(q, k, v, window, dil):
    B, S, H, Dh = q.shape
    bw = window // dil
    n = S // dil
    nb = -(-n // bw)
    pad = nb * bw - n

    def sub(t):
        t = t.reshape(B, n, dil, H, Dh).transpose(0, 2, 1, 3, 4)
        return jnp.pad(t, ((0, 0), (0, 0), (0, pad), (0, 0), (0, 0)))

    def band(t):
        tp = jnp.pad(t, ((0, 0), (0, 0), (bw, 0), (0, 0), (0, 0)))
        prev = tp[:, :, :nb * bw].reshape(B, dil, nb, bw, H, Dh)
        cur = t.reshape(B, dil, nb, bw, H, Dh)
        return jnp.concatenate([prev, cur], axis=3)

    qb = sub(q).reshape(B, dil, nb, bw, H, Dh).astype(jnp.float32)
    kb = band(sub(k)).astype(jnp.float32)
    vb = band(sub(v)).astype(jnp.float32)

    r = jnp.arange(bw)[:, None]
    j = jnp.arange(2 * bw)[None, :]
    diff = bw + r - j
    kidx = (jnp.arange(nb)[:, None, None] - 1) * bw + j[None]
    mask = (diff >= 0) & (diff <= bw) & (kidx >= 0)

    s = jnp.einsum('bgiqhd,bgikhd->bgihqk', qb, kb) * (Dh ** -0.5)
    s = jnp.where(mask[None, None, :, None], s, -jnp.inf)
    m = jnp.max(s, axis=-1, keepdims=True)
    p = jnp.exp(s - m)
    l = jnp.sum(p, axis=-1, keepdims=True)
    o = jnp.einsum('bgihqk,bgikhd->bgiqhd', p, vb) / jnp.swapaxes(l, 3, 4)
    lse = jnp.swapaxes((m + jnp.log(l))[..., 0], 3, 4)

    o = o.reshape(B, dil, nb * bw, H, Dh)[:, :, :n].transpose(0, 2, 1, 3, 4).reshape(B, S, H, Dh)
    lse = lse.reshape(B, dil, nb * bw, H)[:, :, :n].transpose(0, 2, 1, 3).reshape(B, S, H)
    return o, lse

def hgrn2_chunkwise(q, k, v, log_f):
    B, S, H, DK = q.shape
    DV = v.shape[-1]
    C = HGRN_CHUNK
    nc = S // C

    def chunk(t):
        return t.astype(jnp.float32).reshape(B, nc, C, H, t.shape[-1]).transpose(0, 3, 1, 2, 4)

    q, k, v, log_f = chunk(q), chunk(k), chunk(v), chunk(log_f)
    b = jnp.cumsum(log_f, axis=3)
    qe = q * jnp.exp(b)
    ke = k * jnp.exp(-b)
    causal = jnp.tril(jnp.ones((C, C), dtype=bool))
    a = jnp.where(causal, jnp.einsum('bhncd,bhnsd->bhncs', qe, ke), 0.0)
    o_intra = jnp.einsum('bhncs,bhnse->bhnce', a, v)

    b_last = b[:, :, :, -1:, :]
    delta = jnp.einsum('bhncd,bhnce->bhnde', k * jnp.exp(b_last - b), v)
    decay = jnp.exp(b_last[:, :, :, 0, :])

    def step(state, inp):
        dec, dl = inp
        return dec[..., None] * state + dl, state

    s0 = jnp.zeros((B, H, DK, DV), jnp.float32)
    _, s_prev = lax.scan(step, s0, (jnp.moveaxis(decay, 2, 0), jnp.moveaxis(delta, 2, 0)))
    s_prev = jnp.moveaxis(s_prev, 0, 2)
    o_inter = jnp.einsum('bhncd,bhnde->bhnce', qe, s_prev)
    return (o_intra + o_inter).transpose(0, 2, 3, 1, 4).reshape(B, S, H, DV)

def hybrid_mixer(h, w_in, attn_norm_w, lb, hgrn_norm_w, w_out):
    B, S, _ = h.shape
    proj = h @ w_in
    widths = [D_ATTN, D_ATTN, D_ATTN, D_FORGET, D_FORGET, D_REC, D_REC]
    cuts = [int(v) for v in np.cumsum(widths)[:-1]]
    qa, ka, va, qr, fr, ir, gr = jnp.split(proj, cuts, axis=-1)

    qa = qa.reshape(B, S, N_HEADS_A, HEAD_DIM_A)
    ka = ka.reshape(B, S, N_HEADS_A, HEAD_DIM_A)
    va = va.reshape(B, S, N_HEADS_A, HEAD_DIM_A)
    outs, lses = [], []
    for window, dil in DILATED_PAIRS:
        o, lse = dilated_causal_attention(qa, ka, va, window, dil)
        outs.append(o)
        lses.append(lse)
    wts = jax.nn.softmax(jnp.stack(lses, axis=0), axis=0)
    o_a = jnp.einsum('nbsh,nbshd->bshd', wts, jnp.stack(outs, axis=0)).astype(h.dtype)
    y_a = rms_norm_2(o_a, attn_norm_w.reshape(N_HEADS_A, HEAD_DIM_A)).reshape(B, S, D_ATTN)

    q_r = jax.nn.silu(qr.astype(jnp.float32)).reshape(B, S, N_HEADS_R, HGRN_EXPAND)
    lb_h = lb.reshape(N_HEADS_R, HGRN_EXPAND)
    f = lb_h + (1.0 - lb_h) * jax.nn.sigmoid(fr.astype(jnp.float32).reshape(B, S, N_HEADS_R, HGRN_EXPAND))
    v_r = ir.reshape(B, S, N_HEADS_R, HEAD_DIM_R)
    o_r = hgrn2_chunkwise(q_r, 1.0 - f, v_r, jnp.log(f)).astype(h.dtype)
    o_r = rms_norm_2(o_r, hgrn_norm_w.reshape(N_HEADS_R, HEAD_DIM_R)).reshape(B, S, D_REC)
    y_r = o_r * jax.nn.silu(gr)

    return jnp.concatenate([y_a, y_r], axis=-1) @ w_out

def moe_ffn(h, w_router, b_router, w_gu, b_gu, w_down, b_down):
    B, S, D = h.shape
    T = B * S
    ht = h.reshape(T, D)
    logits = (ht @ w_router + b_router).astype(jnp.float32)
    top_val, top_idx = lax.top_k(logits, TOP_K)
    gates = jax.nn.softmax(top_val, axis=-1)

    flat_e = top_idx.reshape(-1)
    flat_tok = jnp.arange(T * TOP_K, dtype=jnp.int32) // TOP_K
    flat_gate = gates.reshape(-1)
    order = jnp.argsort(flat_e)
    se, stok, sgate = flat_e[order], flat_tok[order], flat_gate[order]
    counts = jnp.zeros((N_EXPERTS,), jnp.int32).at[flat_e].add(1)
    padded = ((counts + MOE_BLOCK - 1) // MOE_BLOCK) * MOE_BLOCK
    pend = jnp.cumsum(padded)
    pstart = pend - padded
    sstart = jnp.cumsum(counts) - counts
    rank = jnp.arange(T * TOP_K, dtype=jnp.int32) - sstart[se]
    dest = pstart[se] + rank
    P = T * TOP_K + N_EXPERTS * MOE_BLOCK
    nblk = P // MOE_BLOCK
    tok_pad = jnp.full((P,), T, jnp.int32).at[dest].set(stok)
    gate_pad = jnp.zeros((P,), h.dtype).at[dest].set(sgate.astype(h.dtype))
    blk_e = jnp.minimum(jnp.searchsorted(pend, jnp.arange(nblk) * MOE_BLOCK, side='right'),
                        N_EXPERTS - 1).astype(jnp.int32)
    x_pad = jnp.concatenate([ht, jnp.zeros((1, D), ht.dtype)], axis=0)
    xb = x_pad[tok_pad].reshape(nblk, MOE_BLOCK, D)

    def expert_block(args):
        xblk, e = args
        hg = xblk @ w_gu[e] + b_gu[e]
        x_glu, x_lin = hg[:, :D_FF], hg[:, D_FF:]
        x_glu = jnp.minimum(x_glu, SWIGLU_LIMIT)
        x_lin = jnp.clip(x_lin, -SWIGLU_LIMIT, SWIGLU_LIMIT)
        act = x_glu * jax.nn.sigmoid(SWIGLU_ALPHA * x_glu) * (x_lin + 1.0)
        return act @ w_down[e] + b_down[e]

    yb = lax.map(expert_block, (xb, blk_e))
    y = yb.reshape(P, D) * gate_pad[:, None]
    out = jnp.zeros((T + 1, D), y.dtype).at[tok_pad].add(y)[:T]
    return out.reshape(B, S, D)

def second_inputs(seed: int = 0) -> dict:
    key = jax.random.key(seed)
    ks = jax.random.split(key, 20)

    def nrm(k, shape, scale):
        return jax.random.normal(k, shape, jnp.float32) * scale

    return {
        "x": nrm(ks[0], (BATCH, SEQ, D_MODEL), 1.0),
        "c": nrm(ks[1], (BATCH, D_MODEL), 1.0),
        "w_ada": nrm(ks[2], (DEPTH_2, D_MODEL, 6 * D_MODEL), 0.5 * D_MODEL ** -0.5),
        "b_ada": nrm(ks[3], (DEPTH_2, 6 * D_MODEL), 0.02),
        "g_pre_mix": 1.0 + nrm(ks[4], (DEPTH_2, D_MODEL), 0.05),
        "g_post_mix": 1.0 + nrm(ks[5], (DEPTH_2, D_MODEL), 0.05),
        "w_in": nrm(ks[6], (DEPTH_2, D_MODEL, D_IN), D_MODEL ** -0.5),
        "attn_norm_w": 1.0 + nrm(ks[7], (DEPTH_2, D_ATTN), 0.05),
        "hgrn_lb": nrm(ks[8], (DEPTH_2 + 1, D_FORGET), 0.5),
        "hgrn_norm_w": 1.0 + nrm(ks[9], (DEPTH_2, D_REC), 0.05),
        "w_out": nrm(ks[10], (DEPTH_2, D_MODEL, D_MODEL), D_MODEL ** -0.5),
        "g_pre_ffn": 1.0 + nrm(ks[11], (DEPTH_2, D_MODEL), 0.05),
        "g_post_ffn": 1.0 + nrm(ks[12], (DEPTH_2, D_MODEL), 0.05),
        "w_router": nrm(ks[13], (DEPTH_2, D_MODEL, N_EXPERTS), D_MODEL ** -0.5),
        "b_router": nrm(ks[14], (DEPTH_2, N_EXPERTS), 0.01),
        "w_gu": nrm(ks[15], (DEPTH_2, N_EXPERTS, D_MODEL, 2 * D_FF), D_MODEL ** -0.5),
        "b_gu": nrm(ks[16], (DEPTH_2, N_EXPERTS, 2 * D_FF), 0.02),
        "w_down": nrm(ks[17], (DEPTH_2, N_EXPERTS, D_FF, D_MODEL), D_FF ** -0.5),
        "b_down": nrm(ks[18], (DEPTH_2, N_EXPERTS, D_MODEL), 0.02),
    }

def second_block(x, c, w_ada, b_ada, g_pre_mix, g_post_mix, w_in, attn_norm_w, hgrn_lb,
              hgrn_norm_w, w_out, g_pre_ffn, g_post_ffn, w_router, b_router, w_gu, b_gu,
              w_down, b_down):
    lb_table = jnp.cumsum(jax.nn.softmax(hgrn_lb.astype(jnp.float32), axis=0), axis=0)
    cond = jax.nn.silu(c)
    for l in range(DEPTH_2):
        mod = cond @ w_ada[l] + b_ada[l]
        shift_m, scale_m, gate_m, shift_f, scale_f, gate_f = jnp.split(mod, 6, axis=-1)
        h = modulate_2(rms_norm_2(x, g_pre_mix[l]), shift_m, scale_m)
        y = hybrid_mixer(h, w_in[l], attn_norm_w[l], lb_table[l], hgrn_norm_w[l], w_out[l])
        x = x + gate_m[:, None, :] * rms_norm_2(y, g_post_mix[l])
        h = modulate_2(rms_norm_2(x, g_pre_ffn[l]), shift_f, scale_f)
        y = moe_ffn(h, w_router[l], b_router[l], w_gu[l], b_gu[l], w_down[l], b_down[l])
        x = x + gate_f[:, None, :] * rms_norm_2(y, g_post_ffn[l])
    return x


def setup_inputs(seed=0):
    out = dict(first_inputs(seed))
    for name, value in second_inputs(seed + 1).items():
        if name != "x":
            out[name + "_2"] = value
    return out


def reference(
    x, c, ctx, c_ctx, mod_w, mod_b, norm1_g, norm2_g, ev_w_in, ev_w_out, sc_conv_w, da_q_norm,
    da_k_norm, da_lq1, da_lk1, da_lq2, da_lk2, da_subln_g, od_w_in, od_w_out, pool_w,
    pool_scale, ret_decay_f, ret_decay_b, ret_gn_g, ffn_w_up, ffn_conv_w, ffn_conv_b,
    ffn_w_down, c_2, w_ada_2, b_ada_2, g_pre_mix_2, g_post_mix_2, w_in_2, attn_norm_w_2,
    hgrn_lb_2, hgrn_norm_w_2, w_out_2, g_pre_ffn_2, g_post_ffn_2, w_router_2, b_router_2,
    w_gu_2, b_gu_2, w_down_2, b_down_2,
):
    x = first_block(
        x, c, ctx, c_ctx, mod_w, mod_b, norm1_g, norm2_g, ev_w_in, ev_w_out, sc_conv_w,
        da_q_norm, da_k_norm, da_lq1, da_lk1, da_lq2, da_lk2, da_subln_g, od_w_in, od_w_out,
        pool_w, pool_scale, ret_decay_f, ret_decay_b, ret_gn_g, ffn_w_up, ffn_conv_w,
        ffn_conv_b, ffn_w_down,
    )
    return second_block(
        x, c_2, w_ada_2, b_ada_2, g_pre_mix_2, g_post_mix_2, w_in_2, attn_norm_w_2, hgrn_lb_2,
        hgrn_norm_w_2, w_out_2, g_pre_ffn_2, g_post_ffn_2, w_router_2, b_router_2, w_gu_2,
        b_gu_2, w_down_2, b_down_2,
    )


_drawn_inputs = setup_inputs


def setup_inputs(seed=0):
    import zlib

    import numpy as np

    out = dict(_drawn_inputs(seed))
    spreads = {}
    factors = {'da_q_norm': 5.52,
     'da_k_norm': 4.811,
     'da_lq1': 7.666,
     'da_lk1': 8.0,
     'da_lq2': 6.449,
     'da_lk2': 8.0,
     'da_subln_g': 2.728,
     'pool_scale': 3.641,
     'ret_gn_g': 6.269,
     'ffn_conv_b': 8.0,
     'g_post_mix_2': 2.937,
     'attn_norm_w_2': 2.945,
     'hgrn_lb_2': 3.703,
     'hgrn_norm_w_2': 6.402,
     'g_post_ffn_2': 4.393,
     'b_router_2': 4.231,
     'b_gu_2': 8.0,
     'b_down_2': 8.0}
    for name, (base, spread) in spreads.items():
        noise = np.random.default_rng([zlib.crc32(name.encode()), seed]).standard_normal(out[name].shape)
        drawn = base * np.exp(spread * noise) if base else spread * noise
        out[name] = __import__('jax').numpy.asarray(drawn.astype(out[name].dtype))
    for name, factor in factors.items():
        out[name] = (out[name] * factor).astype(out[name].dtype)
    return out
```

```python
from contextlib import ExitStack

import numpy as np

import concourse.bass as bass
from concourse import mybir

ALU = mybir.AluOpType
ACT = mybir.ActivationFunctionType
AX = mybir.AxisListType
F32 = mybir.dt.float32
I32 = mybir.dt.int32

P = 128
D = 1024
DC = D // P
S = 256
T2 = 512
FFN = 2816
FC = FFN // P
EPS = 1e-6
LAM0 = 0.2
NE = 32
CAP = 64
MAXB = S * 4 // CAP + NE
RING = 12
SLOT = 2048
GUC = 8
HC = 32

VEC = [("cin", 16), ("c2", 8), ("mod_b0", 48), ("mod_b1", 48), ("mod_b2", 48),
       ("n1_0", 8), ("n2_0", 8), ("n1_1", 8), ("n2_1", 8), ("scw", 12), ("qg", 1), ("kg", 1),
       ("lq1", 1), ("lk1", 1), ("lq2", 1), ("lk2", 1), ("subln", 1),
       ("pscale", 4), ("decf", 4), ("decb", 4), ("gng", 1),
       ("fcw_0", 66), ("fcw_1", 66), ("fcb_0", 22), ("fcb_1", 22),
       ("gpm", 8), ("gqm", 8), ("anw", 4), ("hlb", 8), ("hnw", 4), ("gpf", 8), ("gqf", 8),
       ("bgu", 512), ("bdn", 256)]
TAB = [("ident", 128), ("ones", 256), ("bd64", 128), ("rot", 128), ("cos", 256), ("sin", 256),
       ("tri", 128), ("hmask", 128), ("rbase", 256), ("iota", CAP), ("bidx", MAXB + 1),
       ("hreset", 256), ("eps", 1)]
LATE = [("cnt", 512), ("neg", 512), ("invc", 1024)]


def offsets(spec):
    at, out = 0, {}
    for name, n in spec:
        out[name] = (at, n)
        at += n
    return out, at


VOFF, NV = offsets(VEC)
TOFF, NT = offsets(TAB)


def tables():
    t = {}
    p = np.arange(P)
    t["ident"] = np.eye(P)
    t["ones"] = np.ones((P, 2 * P))
    t["bd64"] = (p[:, None] // 64 == p[None] // 64)
    rot = np.zeros((P, P))
    for m in range(P):
        if (m % 32) < 16:
            rot[m + 16, m] = -1.0
        else:
            rot[m - 16, m] = 1.0
    t["rot"] = rot
    tok = np.arange(S)
    inv = np.float32(10000.0) ** (-np.arange(16, dtype=np.float32) / np.float32(16))
    pos = np.stack([tok // 64, tok % 64]).astype(np.float32)
    ang = pos[(p % 64) // 32] * inv[p % 16][:, None].astype(np.float32)
    t["cos"], t["sin"] = np.cos(ang), np.sin(ang)
    t["tri"] = p[:, None] < p[None]
    t["hmask"] = (p[:, None] // HC == p[None] // HC) & (p[:, None] <= p[None])
    q = np.arange(S)
    d = q[:, None] - q[None]
    cnt = ((d >= 0) & (d <= 128)).astype(np.float32) + ((d >= 0) & (d % 4 == 0)) + ((d >= 0) & (d % 16 == 0))
    cnt = cnt.reshape(2, P, S).transpose(1, 0, 2)
    t["cnt"] = cnt.reshape(P, -1)
    t["neg"] = np.where(cnt > 0, 0.0, -1e30).reshape(P, -1)
    t["rbase"] = q[None] - p[:, None]
    invc = np.stack([1.0 / (np.minimum(q + r + 1, S) - np.maximum(q - r, 0)) for r in (1, 2, 4, 8)])
    t["invc"] = np.broadcast_to(invc.reshape(1, -1), (P, 4 * S))
    t["iota"] = np.broadcast_to(np.arange(CAP), (P, CAP))
    t["bidx"] = np.broadcast_to(np.arange(MAXB + 1), (P, MAXB + 1))
    t["hreset"] = np.broadcast_to((q % HC != 0), (P, S))
    t["eps"] = np.full((P, 1), EPS)
    return [np.ascontiguousarray(np.concatenate([np.asarray(t[n], np.float32).reshape(P, w) for n, w in spec], axis=1))
            for spec in (TAB, LATE)]


def program(nc, xin, vec, tab, late, brouter, mod_w, ev_w_in, ev_w_out, od_w_in, od_w_out, pool_w,
            ffn_w_up, ffn_w_down, w_ada, w_in2, w_out2, w_router, w_gu, w_down, out):
    with ExitStack() as ctx:
        def sb(name, shape, dt=F32):
            return ctx.enter_context(nc.sbuf_tensor(name, shape, dt))

        def sem(name):
            return ctx.enter_context(nc.semaphore(name))

        wring = sb("wring", [P, RING, SLOT])
        xT = sb("xT", [P, DC, T2])
        hT = sb("hT", [P, DC, T2])
        big = sb("big", [P, 24, T2])
        tmp = sb("tmp", [P, 6, T2])
        vecs = sb("vecs", [P, NV])
        tabs = sb("tabs", [P, NT])
        modv = sb("modv", [P, 3, 48, 2])
        gsc = sb("gsc", [P, 6, DC, 2])
        cs = sb("cs", [P, 24])
        sm = sb("sm", [P, 128])
        brow = sb("brow", [1, NE])
        rows = sb("rows", [2, 2, 256])
        topi = sb("topi", [P, 8], mybir.dt.uint32)
        wr = sb("wr", [P, DC, NE])
        itab = sb("itab", [P, 3, MAXB + 1], I32)
        bank = [ctx.enter_context(nc.psum_tensor(f"bank{i}", [P, 512], F32)) for i in range(8)]

        def V(name, a=0, b=None):
            at, n = VOFF[name]
            return vecs[:, at + a:at + (n if b is None else b)]

        def V1(name, i=0):
            return V(name, i, i + 1)

        def C(name, a=0, b=None):
            at, n = TOFF[name]
            return tabs[:, at + a:at + (n if b is None else b)]

        ident, ones, bd64, rotm = C("ident"), C("ones", 0, P), C("bd64"), C("rot")

        def late_row(i):
            return xT[:, i, S:T2]

        cnt, neg, invc = [[late_row(i) for i in r] for r in (range(2), range(2, 4), range(4, 8))]

        def Qh(h):
            return big[:, h, :]

        def Kh(h):
            return big[:, 4 + h, :]

        def Vt(tt):
            return big[:, 8 + tt, :]

        def Yc(j):
            return big[:, 12 + j, :]

        def Oh(h):
            return big[:, 16 + h, :]

        bank_full = [sem(f"bank_full{i}") for i in range(8)]
        bank_free = [sem(f"bank_free{i}") for i in range(8)]
        w_full = [sem(f"w_full{i}") for i in range(RING)]
        w_used = sem("w_used")
        names = {}

        def G(name):
            if name not in names:
                names[name] = sem(name)
            return names[name]

        turn = {}
        turns = [0] * 8
        ringbank = [0]
        stream = []

        def full(eng, key):
            b, n = turn[key]
            eng.wait_ge(bank_full[b], n + 1)
            return bank[b]

        def freed(eng, key):
            b, n = turn[key]
            eng.wait_ge(bank_free[b], n + 1)

        def release(ins, key):
            ins.then_inc(bank_free[turn[key][0]], 1)

        block = ctx.enter_context(nc.Block())

        def colsrc(w, c0, n=256, k0=0, k1=8):
            return (w[128 * k0:128 * k1, c0:c0 + n].rearrange("(k p) n -> p k n", p=P), (k1 - k0) * n)

        UNITS = [(h, qt) for h in range(4) for qt in range(4)]
        A2 = [(h, qt) for h in range(8) for qt in range(2)]
        NORM = [(0, 0, T2), (0, 3, T2), (1, 0, T2), (1, 3, S), (2, 0, S), (2, 3, S)]

        def half(i):
            return big[:, i // 2, S * (i % 2):S * (i % 2) + S]

        RK = [big[:, 0, :], big[:, 1, :]]
        RQ = [big[:, 2, 0:S], big[:, 2, S:T2]]
        RV = [big[:, 3 + i, :] for i in range(4)]
        RG = [big[:, 7 + j // 2, S * (j % 2):S * (j % 2) + S] for j in range(4)]
        RCAT = [big[:, 9 + j // 2, S * (j % 2):S * (j % 2) + S] for j in range(8)]
        RO = [big[:, 13 + j // 2, S * (j % 2):S * (j % 2) + S] for j in range(4)]
        RD = [big[:, 15 + 2 * h:17 + 2 * h, :].rearrange("p a s -> p (a s)") for h in range(4)]
        RS = [half(30 + h) for h in range(4)]
        DISTF = tmp[:, 0:2, :].rearrange("p a s -> p (a s)")
        DISTB = tmp[:, 2:4, :].rearrange("p a s -> p (a s)")
        EXPB = tmp[:, 4:6, :].rearrange("p a s -> p (a s)")
        MASKF, MASKB = big[:, 23, :], big[:, 13, :]
        QA = [half(i) for i in range(4)]
        KA = [half(4 + i) for i in range(4)]
        VA = [big[:, 4 + i, :] for i in range(2)]
        IR = [big[:, 6 + i, :] for i in range(2)]
        QE = [half(16 + i) for i in range(4)]
        KE = [half(20 + i) for i in range(4)]
        KD = [half(24 + i) for i in range(4)]
        GR = [half(28 + i) for i in range(4)]
        CAT2 = [half(32 + i) for i in range(8)]
        OA = QA
        OR = KA
        Y2 = [half(i) for i in range(8)]
        YF = CAT2
        KDT = half(40)
        AM = half(41)
        ST = big[:, 21:23, :].rearrange("p a (n e) -> p (a n) e", e=P)

        def DECAY(h):
            return sm[:, 64 + 8 * h:72 + 8 * h]
        H2 = big[:, 0:4, :].rearrange("p a b -> p (a b)").rearrange("p (t k m) -> p t k m", t=2, k=8)
        XG = big[:, 4, :].rearrange("p (k s) -> p k s", k=8)
        GL = big[:, 5, :]
        LI = big[:, 6, :]
        SI = big[:, 7, :]
        AC = big[:, 8, :].rearrange("p (k s) -> p k s", k=8)
        YT = big[:, 9, :].rearrange("p (k s) -> p k s", k=8)
        YK = big[0:CAP, 10:12, :]
        SGT = big[0:CAP, 12, 0:S]
        SEL = big[:, 12, S:S + 128].rearrange("p (t s) -> p t s", t=2)
        SGS = big[:, 12, S + 128:S + 256].rearrange("p (t s) -> p t s", t=2)
        posn = big[:, 13, 0:64].rearrange("p (t e) -> p t e", t=2)
        le3 = big[:, 22, 0:MAXB + 1]
        gate = big[:, 13, 64:128].rearrange("p (t e) -> p t e", t=2)
        offt = big[:, 13, 128:128 + MAXB + 1]
        lg = big[:, 13, 192:256].rearrange("p (t e) -> p t e", t=2)
        lr = big[:, 13, 256:320].rearrange("p (t e) -> p t e", t=2)
        msk = big[:, 13, 320:384].rearrange("p (t e) -> p t e", t=2)
        cum = big[:, 13, 384:416]
        rt = big[:, 13, 416:512]
        le = big[:, 14:18, :].rearrange("p a b -> p (a b)")[:, 0:(MAXB + 1) * NE].rearrange(
            "p (b e) -> p b e", e=NE)
        le2 = big[:, 18:22, :].rearrange("p a b -> p (a b)")[:, 0:(MAXB + 1) * NE].rearrange(
            "p (b e) -> p b e", e=NE)

        MOE = {}

        @block.tensor
        def _(pe):
            pending = [0]

            def mm(o, l, r, start, stop, inc=None):
                ins = pe.matmul(o, l, r, start=start, stop=stop, skip_group_check=True)
                if inc is not None:
                    ins.then_inc(inc, 1)
                elif pending[0]:
                    ins.then_inc(w_used, 1)
                    pending[0] -= 1
                return ins

            def claim(key, b=None):
                if b is None:
                    b = ringbank[0] % 4
                    ringbank[0] += 1
                turn[key] = (b, turns[b])
                if turns[b]:
                    pe.wait_ge(bank_free[b], turns[b])
                turns[b] += 1
                return bank[b], bank_full[b]

            def slot(src):
                n = len(stream)
                stream.append(src)
                pe.wait_ge(w_full[n % RING], 16 * (n // RING + 1))
                return wring[:, n % RING, :]

            def done():
                pending[0] += 1

            def stat(key, mat, srcs, waits):
                bk, fl = claim(key)
                for i, s in enumerate(srcs):
                    waits(i)
                    last = i == len(srcs) - 1
                    mm(bk[:, 0:s.shape[-1]], mat, s, i == 0, last, fl if last else None)

            def norm(n):
                T = NORM[n][2]
                stat(("stat", n), ones, [hT[:, c, 0:T] for c in range(DC)],
                     lambda c: pe.wait_ge(G("x_squared"), DC * n + c + 1))

            seen = [0]

            def hwait(n, c):
                if DC * n + c + 1 > seen[0]:
                    seen[0] = DC * n + c + 1
                    pe.wait_ge(G("h_ready"), seen[0])

            def modulation(m):
                w = (mod_w[0], mod_w[1], w_ada[0])[m].rearrange("(p t) n -> p t n", t=8)
                wid = 2 if m < 2 else 1

                def turn_rows(s):
                    if s == 0:
                        claim(("mod", m), 7)
                    freed(pe, ("mr", m, s))
                    for i in range(2):
                        j = 2 * s + i
                        ins = pe.transpose(bank[7][:, wid * j:wid * j + wid],
                                           rows[0:wid, s % 2, P * i:P * i + P], C("ident")[0:wid, 0:wid])
                    if s == 23:
                        ins.then_inc(bank_full[7], 1)

                for s in range(24):
                    ws = slot((w[:, :, 256 * s:256 * s + 256], 2048)).rearrange("p (k n) -> p k n", k=8)
                    bk, fl = claim(("mr", m, s))
                    for t in range(8):
                        lhs = cs[:, 2 * t:2 * t + 2] if m < 2 else cs[:, 16 + t:17 + t]
                        mm(bk[0:wid, 0:256], lhs, ws[:, t, :], t == 0, t == 7, fl if t == 7 else None)
                    done()
                    if s:
                        turn_rows(s - 1)
                    yield
                turn_rows(23)

            def project(keys, src, n, T, wait=True, first=0, tok0=0):
                ws = slot(src).rearrange("p (k n) -> p k n", k=8)
                for cc, key in enumerate(keys):
                    bk, fl = claim(key)
                    for k in range(DC):
                        if wait:
                            hwait(n, k)
                        mm(bk[:, 0:T], ws[:, k, P * cc:P * cc + P], hT[:, k, tok0:tok0 + T],
                           k == 0, k == DC - 1, fl if k == DC - 1 else None)
                done()

            def project_rows(tag, w, c0, n, tiles):
                for s in range(2):
                    ws = slot(colsrc(w, c0 + 256 * s)).rearrange("p (k n) -> p k n", k=8)
                    for tt in tiles:
                        bk, fl = claim((tag, s, tt))
                        for k in range(DC):
                            hwait(n, k)
                            mm(bk[:, 0:256], hT[:, k, P * tt:P * tt + P], ws[:, k, :],
                               k == 0, k == DC - 1, fl if k == DC - 1 else None)
                    done()

            def contract(tag, w, srcs, T, waits):
                ng = (len(srcs) + 7) // 8
                for pair in range(4):
                    b2 = [claim((tag, 2 * pair + cc)) for cc in range(2)]
                    for g in range(ng):
                        k0, k1 = 8 * g, min(8 * g + 8, len(srcs))
                        ws = slot(colsrc(w, 256 * pair, 256, k0, k1)).rearrange("p (k n) -> p k n", n=256)
                        for cc in range(2):
                            for k in range(k0, k1):
                                if pair == 0 and cc == 0:
                                    waits(k)
                                last = k == len(srcs) - 1
                                mm(b2[cc][0][:, 0:T], ws[:, k - k0, P * cc:P * cc + P], srcs[k],
                                   k == 0, last, b2[cc][1] if last else None)
                        done()

            def ffn(l, T):
                n = 1 + 2 * l
                norm(n)
                for jj in range(FC // 2):
                    project([("fa", l, 2 * jj + i) for i in range(2)], colsrc(ffn_w_up[l], 256 * jj), n, T)
                    project([("fb", l, 2 * jj + i) for i in range(2)], colsrc(ffn_w_up[l], FFN + 256 * jj), n, T)
                contract(("dn", l), ffn_w_down[l], [big[:, j, 0:T] for j in range(FC)], T,
                         lambda j: freed(pe, ("fb", l, j)))

            pe.wait_ge(G("params"), 64)
            pe.wait_ge(G("cond"), 1)
            for _ in modulation(0):
                pass
            bk, fl = claim("lam")
            pe.wait_ge(G("lam_prod"), 1)
            mm(bk[:, 0:2], ones[0:64, :], sm[0:64, 0:2], True, True, fl)

            norm(0)
            win = ev_w_in[0]
            def qk_stat(c):
                freed(pe, ("qk", c))
                stat(("qks", c), bd64, [tmp[:, c % 2, :]], lambda i: None)
            def qk_rot(c):
                pe.wait_ge(G("qk_norm"), c + 1)
                bk, fl = claim(("rot", c))
                mm(bk[:, 0:S], rotm, big[:, c, 0:S], True, True, fl)
            for c2 in range(4):
                project([("qk", 2 * c2), ("qk", 2 * c2 + 1)], colsrc(win, 1536 + 256 * c2), 0, T2)
                if c2:
                    qk_rot(2 * c2 - 2)
                    qk_rot(2 * c2 - 1)
                qk_stat(2 * c2)
                qk_stat(2 * c2 + 1)
            project_rows("v0", win, 2560, 0, range(4))
            qk_rot(6)
            qk_rot(7)

            def scores(u):
                h, qt = UNITS[u]
                pe.wait_ge(G("qk_rope"), 4 + h + 1)
                k0 = 0 if qt < 2 else S
                for m in range(2):
                    bk, fl = claim(("s", u, m), 4 + m)
                    mm(bk[:, 0:T2 - k0], Qh(h)[64 * m:64 * m + 64, P * qt:P * qt + P],
                       Kh(h)[64 * m:64 * m + 64, k0:T2], True, True, fl)

            def turn_p(u):
                h, qt = UNITS[u]
                nk = 4 if qt < 2 else 2
                pe.wait_ge(G("att_p"), u + 1)
                bk, fl = claim(("pt", u), 6)
                for i in range(nk):
                    ins = pe.transpose(bk[:, P * i:P * i + P], tmp[:, 2 * (u % 2), P * i:P * i + P], ident)
                ins.then_inc(fl, 1)

            def pv(u):
                h, qt = UNITS[u]
                nk = 4 if qt < 2 else 2
                freed(pe, ("pt", u))
                bk, fl = claim(("o", u))
                for i in range(nk):
                    mm(bk[:, 0:P], Vt(4 - nk + i)[:, P * h:P * h + P], tmp[:, 4 + u % 2, P * i:P * i + P],
                       i == 0, i == nk - 1, fl if i == nk - 1 else None)

            gates = []
            for pr in range(2):
                for part in (1, 2, 0):
                    gates.append(([("g", part, 2 * pr), ("g", part, 2 * pr + 1)], 512 * part + 256 * pr))
            mod1 = modulation(1)
            for u in range(len(UNITS) + 2):
                if u < len(UNITS):
                    scores(u)
                if u % 3 == 1 and gates:
                    keys, c0 = gates.pop(0)
                    project(keys, colsrc(win, c0), 0, T2)
                for _ in range(1 + (u % 2)):
                    next(mod1, None)
                if 1 <= u <= len(UNITS):
                    turn_p(u - 1)
                if u >= 2:
                    pv(u - 2)
            for keys, c0 in gates:
                project(keys, colsrc(win, c0), 0, T2)
            for _ in mod1:
                pass
            for h in range(4):
                stat(("os", h), ones, [hT[:, h, :]], lambda i: pe.wait_ge(G("o_squared"), h + 1))
            contract("wo0", ev_w_out[0], [Yc(j) for j in range(4)] + [Oh(h) for h in range(4)], T2,
                     lambda k: freed(pe, ("g", 0, k)) if k < 4 else pe.wait_ge(G("o_normed"), k - 3))
            ffn(0, T2)

            norm(2)
            win = od_w_in[0]
            project([("rk", 0), ("rk", 1)], colsrc(win, 768), 2, T2)
            project([("rq", 0), ("rq", 1)], colsrc(win, 512), 2, S)
            project_rows("v1", win, 1024, 2, range(4))
            for i in range(4):
                key = ("rk", i) if i < 2 else ("rq", i - 2)
                freed(pe, key)
                bk, fl = claim(("rrot", i))
                mm(bk[:, 0:S], rotm, RK[i][:, 0:S] if i < 2 else RQ[i - 2], True, True, fl)
            mod2 = modulation(2)

            def ret_scores(u):
                h, pr = u // 2, u % 2
                q0 = 64 * (h % 2)
                pe.wait_ge(G("r_rope"), 4)
                bk, fl = claim(("ra", u), 4 + u % 2)
                for i in range(2):
                    kt = 2 * pr + i
                    mm(bk[:, S * i:S * i + S], RK[h // 2][q0:q0 + 64, P * kt:P * kt + P],
                       RQ[h // 2][q0:q0 + 64, :], i == 0, i == 1, fl if i == 1 else None)

            def ret_out(h):
                bk, fl = claim(("ro", h))
                for kt in range(4):
                    u = 2 * h + kt // 2
                    freed(pe, ("ra", u))
                    mm(bk[:, 0:S], RV[kt][:, P * h:P * h + P], tmp[:, u % 4, S * (kt % 2):S * (kt % 2) + S],
                       kt == 0, kt == 3, fl if kt == 3 else None)

            for h in range(5):
                if h < 4:
                    ret_scores(2 * h)
                    ret_scores(2 * h + 1)
                if h == 0:
                    project([("rg", 0), ("rg", 1)], colsrc(win, 1536), 2, S)
                    project([("rg", 2), ("rg", 3)], colsrc(win, 1792), 2, S)
                if h == 1:
                    project([("rp", 0), ("rp", 1)], colsrc(win, 0), 2, S)
                    project([("rp", 2), ("rp", 3)], colsrc(win, 256), 2, S)
                for _ in range(4):
                    next(mod2, None)
                if h:
                    ret_out(h - 1)
            for _ in mod2:
                pass
            for h in range(4):
                stat(("ros", h), ones, [hT[:, h, 0:S]], lambda i: freed(pe, ("ro", h)))
            ws = slot((pool_w[0].rearrange("g c d -> c g d"), 512))
            for g in range(4):
                pe.wait_ge(G("pooled"), g + 1)
                bk, fl = claim(("pw", g))
                mm(bk[:, 0:S], ws[:, P * g:P * g + P], RCAT[g], True, True, fl)
            done()
            contract("wo1", od_w_out[0], RCAT, S,
                     lambda k: freed(pe, ("pw", k)) if k < 4 else pe.wait_ge(G("ro_normed"), k - 3))
            ffn(1, S)

            norm(4)
            win = w_in2[0]
            for i in range(2):
                project([("frg", 2 * i), ("frg", 2 * i + 1)], colsrc(win, 2048 + 256 * i), 4, S)
            for i in range(2):
                project([("qr", 2 * i), ("qr", 2 * i + 1)], colsrc(win, 1536 + 256 * i), 4, S)
            for i in range(4):
                project([("a2", 2 * i), ("a2", 2 * i + 1)], colsrc(win, 256 * i), 4, S)
            project_rows("va", win, 1024, 4, range(2))
            project_rows("ir", win, 2560, 4, range(2))

            def a_scores(u):
                h, qt = A2[u]
                q0 = 64 * (h % 2)
                freed(pe, ("a2", 4 + h // 2))
                bk, fl = claim(("as", u), 4 + u % 2)
                mm(bk[:, 0:P * (qt + 1)], QA[h // 2][q0:q0 + 64, P * qt:P * qt + P],
                   KA[h // 2][q0:q0 + 64, 0:P * (qt + 1)], True, True, fl)

            def a_turn(u):
                h, qt = A2[u]
                pe.wait_ge(G("a_p"), u + 1)
                bk, fl = claim(("apt", u), 6)
                for i in range(qt + 1):
                    ins = pe.transpose(bk[:, P * i:P * i + P], tmp[:, u % 2, P * i:P * i + P], ident)
                ins.then_inc(fl, 1)

            def a_pv(u):
                h, qt = A2[u]
                q0 = 64 * (h % 2)
                freed(pe, ("apt", u))
                bk, fl = claim(("ao", u))
                for i in range(qt + 1):
                    mm(bk[q0:q0 + 64, 0:P], VA[i][:, 64 * h:64 * h + 64],
                       tmp[:, 2 + u % 2, P * i:P * i + P], i == 0, i == qt, fl if i == qt else None)

            def hgrn_turn(h):
                pe.wait_ge(G("g_ready"), h + 1)
                bk, fl = claim(("kdt", h), 7)
                for tt in range(2):
                    ins = pe.transpose(bk[:, P * tt:P * tt + P], KD[h][:, P * tt:P * tt + P], ident)
                ins.then_inc(fl, 1)

            def hgrn_in(h):
                bk, fl = claim(("am", h), 7)
                for tt in range(2):
                    mm(bk[:, P * tt:P * tt + P], KE[h][:, P * tt:P * tt + P], QE[h][:, P * tt:P * tt + P],
                       tt == 0, tt == 1, fl if tt else None)
                freed(pe, ("kdt", h))
                for g in range(4):
                    bk, fl = claim(("dl", h, g))
                    ns = [n for n in (g, g + 4) if n < 7]
                    for n in ns:
                        mm(bk[:, P * (n // 4):P * (n // 4) + P], KDT[HC * g:HC * g + HC, P * (n // 4):P * (n // 4) + P],
                           IR[n // 4][HC * g:HC * g + HC, P * h:P * h + P], n == g, True,
                           fl if n == ns[-1] else None)

            def hgrn_out(h):
                freed(pe, ("am", h))
                pe.wait_ge(G("states"), h + 1)
                bk, fl = claim(("or", h))
                for tt in range(2):
                    mm(bk[:, P * tt:P * tt + P], IR[tt][:, P * h:P * h + P], AM[:, P * tt:P * tt + P],
                       tt == 0, False)
                for n in range(1, 8):
                    mm(bk[:, HC * n:HC * n + HC], ST[:, n, :], QE[h][:, HC * n:HC * n + HC],
                       False, n == 7, fl if n == 7 else None)

            for u in range(len(A2) + 2):
                if u < len(A2):
                    a_scores(u)
                if u == 1:
                    project([("grg", 0), ("grg", 1)], colsrc(win, 3072), 4, S)
                if u == 2:
                    project([("grg", 2), ("grg", 3)], colsrc(win, 3328), 4, S)
                if 1 <= u <= len(A2):
                    a_turn(u - 1)
                if u >= 2:
                    a_pv(u - 2)
            for h in range(4):
                hgrn_turn(h)
                hgrn_in(h)
                hgrn_out(h)
            for c in range(4):
                stat(("as2", c), bd64, [hT[:, c, 0:S]], lambda i: freed(pe, ("ao", 4 * c + 3)))
            for h in range(4):
                stat(("or2", h), ones, [hT[:, 4 + h, 0:S]], lambda i: freed(pe, ("or", h)))
            contract("wo2", w_out2[0], CAT2, S, lambda k: pe.wait_ge(G("cat2"), k + 1))
            stat("post", ones, [hT[:, c, 0:S] for c in range(DC)], lambda c: freed(pe, ("wo2", c)))

            norm(5)
            for tt in range(2):
                bk, fl = claim(("lg", tt))
                for k in range(DC):
                    hwait(5, k)
                    mm(bk[:, 0:NE], hT[:, k, P * tt:P * tt + P], wr[:, k, :], k == 0, False)
                mm(bk[:, 0:NE], ones[0:1, :], brow[0:1, :], False, True, fl)
            for tt in range(2):
                for g in range(2):
                    bk, fl = claim(("h2", tt, g), 6)
                    for i in range(4):
                        ins = pe.transpose(bk[:, P * i:P * i + P], hT[:, 4 * g + i, P * tt:P * tt + P], ident)
                    ins.then_inc(fl, 1)
            pe.wait_ge(G("mask"), 2)
            for tt in range(2):
                bk, fl = claim(("rank", tt))
                mm(bk[:, 0:NE], C("tri"), msk[:, tt, :], True, tt == 0, fl if tt == 0 else None)
                if tt:
                    mm(bk[:, 0:NE], ones, msk[:, 0, :], False, True, fl)
            bk, fl = claim("count")
            for tt in range(2):
                mm(bk[:, 0:NE], ones, msk[:, tt, :], tt == 0, tt == 1, fl if tt else None)

            pe.wait_ge(G("zeroed"), 1)
            for i in range(4):
                bk, fl = claim(("acc", i), i)
                mm(bk[:, :], big[:, 23, 0:P], tabs[:, 0:512], True, True)

            base = len(stream)
            MOE["slot0"] = base
            MOE["turns"] = list(turns)
            t4, t5, t6, t7 = turns[4:8]

            def wslot(s, e):
                n = base + s
                pe.wait_ge(w_full[n % RING], e * 16 + 16 * (n // RING + 1))
                return wring[:, n % RING, :]

            def xmm(o, l, r, start, stop, inc=None):
                ins = pe.matmul(o, l, r, start=start, stop=stop, skip_group_check=True)
                if inc is not None:
                    ins.then_inc(inc, 1)

            def gather(n, b1, inc):
                pe.wait_ge(G("sel"), b1)
                pe.wait_ge(bank_free[6], n)
                for k in range(DC):
                    for tt in range(2):
                        last = k == DC - 1 and tt == 1
                        xmm(bank[6][:, CAP * k:CAP * k + CAP], H2[:, tt, k, :], SEL[:, tt, :],
                            k == 0 and tt == 0, tt == 1,
                            bank_full[6] if last else inc if (k == 0 and tt == 0) else None)

            def gate_up(ts, e, nfree, first=None, early=()):
                for t in ts:
                    ws = wslot(t, e)
                    for j in range(16):
                        bk = bank[4 + j // 8]
                        if t == 0 and j % 8 == 0:
                            pe.wait_ge(bank_free[4 + j // 8], nfree[j // 8])
                        if t == ts[-1] and j == 13:
                            for sm_, n in early:
                                pe.wait_ge(sm_, n)
                        jj = j % 8
                        inc = None
                        if t == 7 and jj == 7:
                            inc = bank_full[4 + j // 8]
                        elif t < 7 and j == 15:
                            inc = G("moe_used")
                        elif t == 0 and j == 0:
                            inc = first
                        xmm(bk[:, CAP * jj:CAP * jj + CAP], ws[:, P * j:P * j + P], XG[:, t, :],
                            t == 0 and jj == 0, t == 7, inc)

            def down(e, n7, b1):
                pe.wait_ge(G("moe_act"), b1)
                pe.wait_ge(bank_free[7], n7)
                for s in range(4):
                    ws = wslot(GUC + s, e).rearrange("p (j n) -> p j n", j=2)
                    for i in range(2):
                        for c in range(DC):
                            k = 2 * s + i
                            last = i == 1 and c == DC - 1
                            xmm(bank[7][:, CAP * c:CAP * c + CAP], ws[:, i, P * c:P * c + P], AC[:, k, :],
                                k == 0 and c == 0, k == 7,
                                (bank_full[7] if s == 3 else G("moe_used")) if last else None)

            def turn_y():
                for c in range(DC):
                    ins = pe.transpose(bank[6 + c // 4][0:CAP, P * (c % 4):P * (c % 4) + P], YT[:, c, :], ident)
                    if c % 4 == 3:
                        ins.then_inc(bank_full[6 + c // 4], 1)

            def turn_g():
                for tt in range(2):
                    ins = pe.transpose(bank[6][0:CAP, P * tt:P * tt + P], SGS[:, tt, :], ident)
                ins.then_inc(bank_full[6], 1)

            def scatter(ny6, ny7, inc=None):
                pe.wait_ge(bank_free[6], ny6)
                pe.wait_ge(bank_free[7], ny7)
                for c in range(DC):
                    xmm(bank[c // 2][:, S * (c % 2):S * (c % 2) + S],
                        YK[:, c // 4, P * (c % 4):P * (c % 4) + P], SGT, False, False, None if c < DC - 1 else inc)

            pe.wait_ge(G("tables"), 2)
            gather(t6, 1, None)
            nblk = pe.value_load(itab[0:1, 2, MAXB:MAXB + 1], min_val=NE, max_val=MAXB - 1)
            pe.wait_ge(bank_free[6], t6 + 1)
            gate_up(range(8), 0, (t4, t5))
            gather(t6 + 1, 2, G("moe_used"))
            down(0, t7, 1)
            with pe.Fori(1, nblk) as b:
                e = pe.value_load(itab[0:1, 0, bass.ds(b, 1)], min_val=0, max_val=NE - 1)
                pe.wait_ge(bank_free[6], b * 3 + (t6 - 1))
                gate_up([0], e, (b + t4, b + t5), G("moe_used"), [(bank_free[7], b * 2 + (t7 - 1))])
                turn_y()
                gate_up(range(1, 4), e, None, None, [(bank_free[6], b * 3 + t6), (G("gsel"), b)])
                turn_g()
                gate_up(range(4, 8), e, None)
                gather(b * 3 + (t6 + 1), b + 2, G("moe_used"))
                scatter(b * 3 + (t6 + 1), b * 2 + t7)
                down(e, b * 2 + t7, b + 1)
            pe.wait_ge(G("loop_end"), 2)
            turn_y()
            pe.wait_ge(G("rows_last"), 1)
            pe.wait_ge(G("gsel_last"), 1)
            turn_g()
            scatter(nblk * 3 + (t6 + 1), nblk * 2 + t7, G("moe_done"))

            for c in range(DC):
                pe.wait_ge(G("fin_sq"), c + 1)
                if c == 0:
                    pe.wait_ge(bank_free[4], nblk + t4)
                mm(bank[4][:, 0:S], ones, hT[:, c, 0:S], c == 0, c == DC - 1, G("fin_stat") if c == DC - 1 else None)

        @block.scalar
        def _(act):
            chain = [0]

            def link(ins):
                chain[0] += 1
                ins.then_inc(G("act_chain"), 1)
                act.wait_ge(G("act_chain"), chain[0])

            def A(o, i, f, **kw):
                return act.activation(o, i, f, **kw)

            def rstd(key, o, n, width):
                bk = full(act, key)
                r = A(o, bk[:, 0:width], ACT.Ln, scale=1.0 / n, bias=C("eps"))
                release(r, key)
                freed(act, key)
                return A(o, o, ACT.Exp, scale=-0.5)

            def norm(n, ready):
                m, part, T = NORM[n]
                for c in range(DC):
                    ready(c)
                    A(hT[:, c, 0:T], xT[:, c, 0:T], ACT.Square).then_inc(G("x_squared"), 1)
                rstd(("stat", n), tmp[:, 0, 0:T], D, T).then_inc(G("rstd"), 1)
                act.wait_ge(G("gsc"), m + 1)
                for c in range(DC):
                    act.wait_ge(G("x_scaled"), DC * n + c + 1)
                    for hf in range(T // S):
                        ins = A(hT[:, c, S * hf:S * hf + S], hT[:, c, S * hf:S * hf + S], ACT.Identity,
                                scale=gsc[:, n, c, hf:hf + 1], bias=modv[:, m, 8 * part + c, hf:hf + 1])
                    ins.then_inc(G("h_ready"), 1)

            def ffn(l, T):
                for j in range(FC):
                    bk = full(act, ("fa", l, j))
                    if j >= 4:
                        freed(act, ("fb", l, j - 4))
                    A(tmp[:, j % 4, 0:T], bk[:, 0:T], ACT.Identity, scale=V1(f"fcw_{l}", FC + j),
                      bias=V1(f"fcb_{l}", j)).then_inc(G("ffn_mid"), 1)
                    if j % 2:
                        for i in (j - 1, j):
                            freed(act, ("fa", l, i))
                            A(tmp[:, i % 4, 0:T], tmp[:, i % 4, 0:T], ACT.Silu).then_inc(G("ffn_silu"), 1)

            def take_rows(m, s):
                bk = full(act, ("mr", m, s))
                w = 2 if m < 2 else 1
                release(A(rows[0:w, s % 2, :], bk[0:w, 0:256], ACT.Copy), ("mr", m, s))

            act.dma_start(vecs[:, :], vec).then_inc(G("params"), 16)
            act.dma_start(tabs[:, :], tab).then_inc(G("params"), 16)
            act.dma_start(wr[:, :, :], w_router[0].rearrange("(k p) e -> p k e", p=P)).then_inc(G("params"), 16)
            act.dma_start(brow[:, :], brouter).then_inc(G("params"), 16)
            act.wait_ge(G("params"), 64)
            A(cs[:, 0:24], vecs[:, 0:24], ACT.Silu).then_inc(G("cond"), 1)
            for s in range(24):
                take_rows(0, s)
            bk = full(act, "lam")
            release(A(sm[:, 2:4], bk[:, 0:2], ACT.Exp), "lam")

            act.wait_ge(G("x_loaded"), 16)
            norm(0, lambda c: None)

            def qk_rstd(c):
                if c >= 2:
                    act.wait_ge(G("qk_norm"), c - 1)
                rstd(("qks", c), tmp[:, 2 + c % 2, :], 64, T2).then_inc(G("qk_rstd"), 1)

            for c in range(8):
                bk = full(act, ("qk", c))
                if c >= 2:
                    full(act, ("qks", c - 2))
                A(big[:, c, :], bk[:, :], ACT.Copy)
                release(A(tmp[:, c % 2, :], bk[:, :], ACT.Square), ("qk", c))
                if c % 2:
                    qk_rstd(c - 1)
                    qk_rstd(c)
            for s in range(2):
                for tt in range(4):
                    bk = full(act, ("v0", s, tt))
                    release(A(Vt(tt)[:, 256 * s:256 * s + 256], bk[:, 0:256], ACT.Copy), ("v0", s, tt))

            def exps(u):
                h, qt = UNITS[u]
                w = T2 if qt < 2 else S
                act.wait_ge(G("att_max"), u + 1)
                if u >= 2:
                    full(act, ("pt", u - 2))
                for m in range(2):
                    bk = full(act, ("s", u, m))
                    release(A(tmp[:, 2 * (u % 2) + m, 0:w], bk[:, 0:w], ACT.Exp, scale=0.125,
                              bias=sm[:, 8 + 8 * (u % 2) + m:9 + 8 * (u % 2) + m],
                              accum_out=sm[:, 10 + 8 * (u % 2) + m:11 + 8 * (u % 2) + m]), ("s", u, m))

            def copy_pt(u):
                h, qt = UNITS[u]
                w = T2 if qt < 2 else S
                bk = full(act, ("pt", u))
                if u >= 2:
                    full(act, ("o", u - 2))
                release(A(tmp[:, 4 + u % 2, 0:w], bk[:, 0:w], ACT.Copy), ("pt", u))

            def copy_o(u):
                h, qt = UNITS[u]
                bk = full(act, ("o", u))
                release(A(Oh(h)[:, P * qt:P * qt + P], bk[:, 0:P], ACT.Copy), ("o", u))

            def copy_c(pr):
                for j in (2 * pr, 2 * pr + 1):
                    bk = full(act, ("g", 1, j))
                    release(A(big[:, 20 + j, :], bk[:, :], ACT.Copy), ("g", 1, j))

            m1 = list(range(24))
            for u in range(len(UNITS) + 2):
                if u < len(UNITS):
                    exps(u)
                if u == 1:
                    copy_c(0)
                if u == 10:
                    copy_c(1)
                for _ in range(1 + (u % 2)):
                    if m1:
                        take_rows(1, m1.pop(0))
                if 1 <= u <= len(UNITS):
                    copy_pt(u - 1)
                if u >= 2:
                    copy_o(u - 2)
            freed(act, ("o", len(UNITS) - 1))
            full(act, ("g", 0, 3))
            for h in range(4):
                A(hT[:, h, :], Oh(h), ACT.Square).then_inc(G("o_squared"), 1)
            for h in range(4):
                rstd(("os", h), tmp[:, h, :], P, T2).then_inc(G("o_rstd"), 1)

            norm(1, lambda c: freed(act, ("wo0", c)))
            ffn(0, T2)

            norm(2, lambda c: freed(act, (("dn", 0), c)))
            act.dma_start(xT[:, :, S:T2], late.rearrange("p (k s) -> p k s", k=DC)).then_inc(G("late_loaded"), 16)
            for i in range(2):
                bk = full(act, ("rk", i))
                release(A(RK[i], bk[:, :], ACT.Copy), ("rk", i))
            for i in range(2):
                bk = full(act, ("rq", i))
                release(A(RQ[i], bk[:, 0:S], ACT.Copy, scale=0.125), ("rq", i))
            for s in range(2):
                for tt in range(4):
                    bk = full(act, ("v1", s, tt))
                    release(A(RV[tt][:, 256 * s:256 * s + 256], bk[:, 0:256], ACT.Copy), ("v1", s, tt))
            link(A(sm[:, 24:32], vecs[:, VOFF["decf"][0]:VOFF["decf"][0] + 8], ACT.Exp))
            link(A(sm[:, 24:32], sm[:, 24:32], ACT.Copy, scale=-1.0))
            act.wait_ge(G("dist"), 1)
            for h in range(4):
                if h:
                    act.wait_ge(G("rd_done"), h)
                A(RD[h], DISTF, ACT.Exp, scale=sm[:, 24 + h:25 + h])
                A(EXPB, DISTB, ACT.Exp, scale=sm[:, 28 + h:29 + h]).then_inc(G("decays"), 1)
            for j in range(4):
                bk = full(act, ("rg", j))
                release(A(RG[j], bk[:, 0:S], ACT.Silu), ("rg", j))
            for s in range(4):
                take_rows(2, s)
            for g in range(4):
                bk = full(act, ("rp", g))
                release(A(RCAT[g], bk[:, 0:S], ACT.Copy), ("rp", g))
            for h in range(4):
                for s in range(4 * h + 4, 4 * h + 8):
                    take_rows(2, s)
                bk = full(act, ("ro", h))
                A(RO[h], bk[:, 0:S], ACT.Copy)
                release(A(hT[:, h, 0:S], bk[:, 0:S], ACT.Square), ("ro", h))
            for s in range(20, 24):
                take_rows(2, s)
            for h in range(4):
                rstd(("ros", h), RS[h], P, S).then_inc(G("ro_rstd"), 1)
            norm(3, lambda c: freed(act, ("wo1", c)))
            ffn(1, S)

            act.wait_ge(G("lb_diff"), 1)
            A(sm[:, 32:36], sm[:, 32:36], ACT.Sigmoid).then_inc(G("lb"), 1)
            norm(4, lambda c: freed(act, (("dn", 1), c)))
            for h in range(4):
                bk = full(act, ("frg", h))
                release(A(KE[h], bk[:, 0:S], ACT.Sigmoid), ("frg", h))
            for h in range(4):
                bk = full(act, ("qr", h))
                release(A(QE[h], bk[:, 0:S], ACT.Silu), ("qr", h))
            for i in range(8):
                bk = full(act, ("a2", i))
                release(A((QA + KA)[i], bk[:, 0:S], ACT.Copy), ("a2", i))
            for tag, dst in (("va", VA), ("ir", IR)):
                for s in range(2):
                    for tt in range(2):
                        bk = full(act, (tag, s, tt))
                        release(A(dst[tt][:, 256 * s:256 * s + 256], bk[:, 0:256], ACT.Copy), (tag, s, tt))
            for h in range(4):
                act.wait_ge(G("forget"), h + 1)
                A(CAT2[h], KD[h], ACT.Ln).then_inc(G("log_f"), 1)
            for h in range(4):
                act.wait_ge(G("scanned"), h + 1)
                A(CAT2[h], CAT2[4 + h], ACT.Exp)
                A(DECAY(h), CAT2[4 + h].rearrange("p (n c) -> p n c", c=HC)[:, :, HC - 1], ACT.Exp)
                link(A(KD[h], KD[h], ACT.Exp))
                A(CAT2[4 + h], CAT2[4 + h], ACT.Exp, scale=-1.0).then_inc(G("exp_b"), 1)

            def a_exp(u):
                h, qt = A2[u]
                w = P * (qt + 1)
                act.wait_ge(G("a_max"), u + 1)
                A(tmp[:, u % 2, 0:w], tmp[:, u % 2, 0:w], ACT.Exp,
                  bias=sm[:, 9 + 4 * (u % 2):10 + 4 * (u % 2)]).then_inc(G("a_exp"), 1)

            def a_copy(u):
                h, qt = A2[u]
                w = P * (qt + 1)
                bk = full(act, ("apt", u))
                if u >= 2:
                    full(act, ("ao", u - 2))
                release(A(tmp[:, 2 + u % 2, 0:w], bk[:, 0:w], ACT.Copy), ("apt", u))

            def a_take(u):
                h, qt = A2[u]
                q0 = 64 * (h % 2)
                bk = full(act, ("ao", u))
                A(OA[h // 2][q0:q0 + 64, P * qt:P * qt + P], bk[q0:q0 + 64, 0:P], ACT.Copy)
                release(A(hT[q0:q0 + 64, h // 2, P * qt:P * qt + P], bk[q0:q0 + 64, 0:P], ACT.Square), ("ao", u))

            for u in range(len(A2) + 2):
                if u < len(A2):
                    a_exp(u)
                if u in (1, 2):
                    for j in (2 * u - 2, 2 * u - 1):
                        bk = full(act, ("grg", j))
                        release(A(GR[j], bk[:, 0:S], ACT.Silu), ("grg", j))
                if 1 <= u <= len(A2):
                    a_copy(u - 1)
                if u >= 2:
                    a_take(u - 2)
            for h in range(4):
                bk = full(act, ("kdt", h))
                if h:
                    full(act, ("dl", h - 1, 3))
                release(A(KDT, bk[:, 0:S], ACT.Copy), ("kdt", h))
                bk = full(act, ("or", h))
                A(OR[h], bk[:, 0:S], ACT.Copy)
                release(A(hT[:, 4 + h, 0:S], bk[:, 0:S], ACT.Square), ("or", h))
            for c in range(4):
                rstd(("as2", c), tmp[:, 4 + c // 2, S * (c % 2):S * (c % 2) + S], 64, S).then_inc(G("as_rstd"), 1)
            for h in range(4):
                rstd(("or2", h), tmp[:, h // 2, S * (h % 2):S * (h % 2) + S], P, S).then_inc(G("or_rstd"), 1)
            for c in range(DC):
                bk = full(act, ("wo2", c))
                A(Y2[c], bk[:, 0:S], ACT.Copy)
                release(A(hT[:, c, 0:S], bk[:, 0:S], ACT.Square), ("wo2", c))
            rstd("post", tmp[:, 0, 0:S], D, S).then_inc(G("post_rstd"), 1)
            norm(5, lambda c: act.wait_ge(G("x_mixed"), c + 1))
            for tt in range(2):
                for g in range(2):
                    bk = full(act, ("h2", tt, g))
                    for i in range(4):
                        c = 4 * g + i
                        ins = A(H2[:, tt, :, 16 * c:16 * c + 16],
                                bk[:, P * i:P * i + P].rearrange("p (m k) -> p k m", k=8), ACT.Copy)
                    release(ins, ("h2", tt, g))
            for tt in range(2):
                act.wait_ge(G("neg_top"), tt + 1)
                A(rt[:, 32 * tt:32 * tt + 32], lg[:, tt, :], ACT.Exp, bias=sm[:, 104 + tt:105 + tt]).then_inc(G("gate_exp"), 1)

            t6 = MOE["turns"][6]

            def take_x(n):
                act.wait_ge(bank_full[6], n)
                A(XG, bank[6][:, :].rearrange("p (k s) -> p k s", k=8), ACT.Copy).then_inc(bank_free[6], 1)

            def sig(b1):
                act.wait_ge(G("glu_in"), b1)
                A(SI, GL, ACT.Sigmoid, scale=1.702).then_inc(G("glu_sig"), 1)

            def take_y(n):
                act.wait_ge(bank_full[6], n)
                A(YK[:, 0, :], bank[6][0:CAP, :], ACT.Copy).then_inc(bank_free[6], 1)

            def take_g(n):
                act.wait_ge(bank_full[6], n)
                A(SGT, bank[6][0:CAP, 0:S], ACT.Copy).then_inc(bank_free[6], 1)

            act.wait_ge(G("tables"), 2)
            nblk = act.value_load(itab[0:1, 2, MAXB:MAXB + 1], min_val=NE, max_val=MAXB - 1)
            take_x(t6 + 1)
            sig(1)
            take_x(t6 + 2)
            with act.Fori(1, nblk) as b:
                take_y(b * 3 + t6)
                take_g(b * 3 + (t6 + 1))
                sig(b + 1)
                take_x(b * 3 + (t6 + 2))
            A(sm[:, 126:127], sm[:, 32:33], ACT.Copy).then_inc(G("loop_end"), 1)
            take_y(nblk * 3 + t6)
            A(sm[:, 126:127], sm[:, 32:33], ACT.Copy).then_inc(G("rows_last"), 1)
            take_g(nblk * 3 + (t6 + 1))
            act.wait_ge(G("moe_done"), 1)
            for c in range(DC):
                A(YF[c], bank[c // 2][:, S * (c % 2):S * (c % 2) + S], ACT.Copy)
                A(hT[:, c, 0:S], bank[c // 2][:, S * (c % 2):S * (c % 2) + S], ACT.Square).then_inc(G("fin_sq"), 1)
            act.wait_ge(G("fin_stat"), 1)
            link(A(tmp[:, 0, 0:S], bank[4][:, 0:S], ACT.Ln, scale=1.0 / D, bias=C("eps")))
            A(tmp[:, 0, 0:S], tmp[:, 0, 0:S], ACT.Exp, scale=-0.5).then_inc(G("fin_rstd"), 1)

        @block.vector
        def _(dve):
            chain = [0]
            v = dve

            def link(ins):
                chain[0] += 1
                ins.then_inc(G("dve_chain"), 1)
                dve.wait_ge(G("dve_chain"), chain[0])

            def TT(o, a, b, op):
                return v.tensor_tensor(o, a, b, op)

            def TS(o, a, s1, s2, op0, op1=None):
                return v.tensor_scalar(o, a, s1, s2, op0, op1) if op1 is not None else v.tensor_scalar(o, a, s1, None, op0)

            def STT(o, a, s1, b, op0, op1):
                return v.scalar_tensor_tensor(o, a, s1, b, op0, op1)

            MUL, ADD, SUB = ALU.mult, ALU.add, ALU.subtract

            def modulation(m):
                w = 2 if m < 2 else 1
                key = ("mod", m)
                bk = full(dve, key)
                release(TT(modv[:, m, :, 0:w], bk[:, 0:48 * w].rearrange("p (j w) -> p j w", w=w),
                           V(f"mod_b{m}").unsqueeze(2).to_broadcast([P, 48, w]), ADD), key)
                freed(dve, key)
                gains = (("n1_0", "n2_0"), ("n1_1", "n2_1"), ("gpm", "gpf"))[m]
                for i in range(2):
                    ins = STT(gsc[:, 2 * m + i, :, 0:w], modv[:, m, 24 * i + 8:24 * i + 16, 0:w], 1.0,
                              V(gains[i]).unsqueeze(2).to_broadcast([P, DC, w]), ADD, MUL)
                ins.then_inc(G("gsc"), 1)

            def norm(n):
                T = NORM[n][2]
                dve.wait_ge(G("rstd"), n + 1)
                for c in range(DC):
                    TT(hT[:, c, 0:T], xT[:, c, 0:T], tmp[:, 0, 0:T], MUL).then_inc(G("x_scaled"), 1)

            def residual(tag, m, part, T):
                for c in range(DC):
                    bk = full(dve, (tag, c))
                    for hf in range(T // S):
                        ins = STT(xT[:, c, S * hf:S * hf + S], bk[:, S * hf:S * hf + S],
                                  modv[:, m, 8 * part + c, hf:hf + 1], xT[:, c, S * hf:S * hf + S], MUL, ADD)
                    release(ins, (tag, c))

            def seg(ap, T):
                return ap[:, 0:T].rearrange("p (g s) -> p g s", s=S)

            def ffn(l, T):
                for j in range(FC):
                    t = seg(tmp[:, j % 4, :], T)
                    bk = seg(full(dve, ("fa", l, j)), T)
                    dve.wait_ge(G("ffn_mid"), FC * l + j + 1)
                    link(STT(t[:, :, 1:S], bk[:, :, 0:S - 1], V1(f"fcw_{l}", j), t[:, :, 1:S], MUL, ADD))
                    release(STT(t[:, :, 0:S - 1], bk[:, :, 1:S], V1(f"fcw_{l}", 2 * FC + j), t[:, :, 0:S - 1],
                                MUL, ADD), ("fa", l, j))
                    if j % 2:
                        for i in (j - 1, j):
                            bk = full(dve, ("fb", l, i))
                            dve.wait_ge(G("ffn_silu"), FC * l + i + 1)
                            release(TT(big[:, i, 0:T], tmp[:, i % 4, 0:T], bk[:, 0:T], MUL), ("fb", l, i))
                residual(("dn", l), l, 5, T)

            dve.wait_ge(G("params"), 64)
            TT(sm[0:64, 0:1], V("lq1")[0:64], V("lk1")[0:64], MUL)
            TT(sm[0:64, 1:2], V("lq2")[0:64], V("lk2")[0:64], MUL).then_inc(G("lam_prod"), 1)
            TT(sm[:, 32:36], V("hlb", 0, 4), V("hlb", 4, 8), SUB).then_inc(G("lb_diff"), 1)
            modulation(0)
            freed(dve, "lam")
            TS(sm[:, 4:5], sm[:, 2:3], sm[:, 3:4], LAM0, SUB, ADD).then_inc(G("lam"), 1)

            norm(0)

            def qk_norm(c):
                dve.wait_ge(G("qk_rstd"), c + 1)
                STT(big[:, c, :], big[:, c, :], V("qg") if c < 4 else V("kg"), tmp[:, 2 + c % 2, :],
                    MUL, MUL).then_inc(G("qk_norm"), 1)

            def turn_pairs(x, t, key):
                bk = full(dve, key)
                release(TT(t, bk[:, 0:S], C("sin"), MUL), key)
                link(TT(x, x, C("cos"), MUL))
                return TT(x, x, t, ADD)

            for c2 in range(5):
                if c2 < 4:
                    qk_norm(2 * c2)
                    qk_norm(2 * c2 + 1)
                if c2:
                    for c in (2 * c2 - 2, 2 * c2 - 1):
                        turn_pairs(big[:, c, 0:S], tmp[:, 4 + c % 2, 0:S], ("rot", c)).then_inc(G("qk_rope"), 1)

            def att_max(u):
                h, qt = UNITS[u]
                w = T2 if qt < 2 else S
                o = 8 + 8 * (u % 2)
                for m in range(2):
                    bk = full(dve, ("s", u, m))
                    ins = v.tensor_reduce(sm[:, o + 6 + m:o + 7 + m], bk[:, 0:w], AX.X, ALU.max)
                link(ins)
                TS(sm[:, o:o + 2], sm[:, o + 6:o + 8], -0.125, None, MUL).then_inc(G("att_max"), 1)

            def att_p(u):
                h, qt = UNITS[u]
                w = T2 if qt < 2 else S
                o = 8 + 8 * (u % 2)
                e0, e1 = tmp[:, 2 * (u % 2), 0:w], tmp[:, 2 * (u % 2) + 1, 0:w]
                freed(dve, ("s", u, 0))
                freed(dve, ("s", u, 1))
                link(v.reciprocal(sm[:, o + 4:o + 6], sm[:, o + 2:o + 4]))
                link(TS(e1, e1, sm[:, o + 5:o + 6], sm[:, 4:5], MUL, MUL))
                STT(e0, e0, sm[:, o + 4:o + 5], e1, MUL, SUB).then_inc(G("att_p"), 1)

            def conv_gates(pr, part):
                for j in (2 * pr, 2 * pr + 1):
                    cx, y = big[:, 20 + j, :], Yc(j)
                    if part == 1:
                        freed(dve, ("g", 1, j))
                        bk = full(dve, ("g", 2, j))
                        release(TT(cx, bk[:, :], cx, MUL), ("g", 2, j))
                        freed(dve, ("g", 2, j))
                        link(TS(y, cx, V1("scw", 4 + j), None, MUL))
                        yy, cc = seg(y, T2), seg(cx, T2)
                        link(STT(yy[:, :, 1:S], cc[:, :, 0:S - 1], V1("scw", j), yy[:, :, 1:S], MUL, ADD))
                        link(STT(yy[:, :, 0:S - 1], cc[:, :, 1:S], V1("scw", 8 + j), yy[:, :, 0:S - 1], MUL, ADD))
                    else:
                        bk = full(dve, ("g", 0, j))
                        release(TT(y, bk[:, :], y, MUL), ("g", 0, j))

            dve.wait_ge(G("lam"), 1)
            for u in range(len(UNITS) + 1):
                if u < len(UNITS):
                    att_max(u)
                if u >= 1:
                    att_p(u - 1)
                if u in (4, 7, 13, 16):
                    conv_gates(u // 10, 1 if u in (4, 13) else 0)
            modulation(1)
            for h in range(4):
                dve.wait_ge(G("o_rstd"), h + 1)
                link(STT(Oh(h), Oh(h), V("subln"), tmp[:, h, :], MUL, MUL))
                TS(Oh(h), Oh(h), 1.0 - LAM0, None, MUL).then_inc(G("o_normed"), 1)
            residual("wo0", 0, 2, T2)
            norm(1)
            ffn(0, T2)

            norm(2)
            dve.wait_ge(G("x_scaled"), 3 * DC)
            for kt in range(2):
                s_ = slice(S * kt, S * kt + S)
                TS(DISTF[:, s_], C("rbase"), -128.0 * kt, 0.0, ADD, ALU.max)
                TS(MASKF[:, s_], C("rbase"), -128.0 * kt, 0.0, ADD, ALU.is_ge)
                TS(MASKB[:, s_], C("rbase"), -128.0 * kt, 0.0, ADD, ALU.is_le)
                link(TS(DISTB[:, s_], C("rbase"), -1.0, 128.0 * kt, MUL, ADD))
                TS(DISTB[:, s_], DISTB[:, s_], 0.0, None, ALU.max)
                c_ = slice(T2 + S * kt, T2 + S * kt + S)
                TS(DISTF[:, c_], C("rbase"), 256.0 - 128.0 * kt, None, ADD)
                ins = TS(DISTB[:, c_], C("rbase"), -1.0, 256.0 + 128.0 * kt, MUL, ADD)
            ins.then_inc(G("dist"), 1)
            for h in range(4):
                dve.wait_ge(G("decays"), h + 1)
                TT(RD[h][:, 0:T2], RD[h][:, 0:T2], MASKF, MUL)
                link(TT(EXPB[:, 0:T2], EXPB[:, 0:T2], MASKB, MUL))
                TT(RD[h], RD[h], EXPB, ADD).then_inc(G("rd_done"), 1)
            dve.wait_ge(G("rd_done"), 4)
            for i in range(4):
                x = RK[i][:, 0:S] if i < 2 else RQ[i - 2]
                turn_pairs(x, EXPB[:, S * i:S * i + S], ("rrot", i)).then_inc(G("r_rope"), 1)
            for u in range(8):
                bk = full(dve, ("ra", u))
                if u == 0:
                    dve.wait_ge(G("rd_done"), 4)
                if u >= 4:
                    full(dve, ("ro", (u - 4) // 2))
                release(TT(tmp[:, u % 4, :], bk[:, :], RD[u // 2][:, T2 * (u % 2):T2 * (u % 2) + T2], MUL), ("ra", u))
            modulation(2)
            dve.wait_ge(G("late_loaded"), 16)
            for g, r in enumerate((1, 2, 4, 8)):
                cs_, w_ = tmp[:, 4, 0:S], tmp[:, 4, S:T2]
                freed(dve, ("rp", g))
                link(v.tensor_tensor_scan(cs_, C("ones"), RCAT[g], 0.0, MUL, ADD))
                v.tensor_copy(w_[:, 0:S - r], cs_[:, r:S])
                link(v.tensor_copy(w_[:, S - r:S], cs_[:, S - 1:S].to_broadcast([P, r])))
                link(TT(w_[:, r + 1:S], w_[:, r + 1:S], cs_[:, 0:S - r - 1], SUB))
                link(TT(w_, w_, invc[g], MUL))
                TT(RCAT[g], w_, RCAT[g], SUB).then_inc(G("pooled"), 1)
            for h in range(4):
                dve.wait_ge(G("ro_rstd"), h + 1)
                link(STT(RO[h], RO[h], V("gng"), RS[h], MUL, MUL))
                TT(RCAT[4 + h], RO[h], RG[h], MUL).then_inc(G("ro_normed"), 1)
            for g in range(4):
                bk = full(dve, ("pw", g))
                release(TS(RCAT[g], bk[:, 0:S], V1("pscale", g), None, MUL), ("pw", g))
            residual("wo1", 1, 2, S)
            norm(3)
            ffn(1, S)

            dve.wait_ge(G("lb"), 1)
            TS(sm[:, 36:40], sm[:, 32:36], -1.0, 1.0, MUL, ADD).then_inc(G("lb_rest"), 1)
            norm(4)
            dve.wait_ge(G("lb_rest"), 1)
            for h in range(4):
                freed(dve, ("frg", h))
                TS(KD[h], KE[h], sm[:, 36 + h:37 + h], sm[:, 32 + h:33 + h], MUL, ADD).then_inc(G("forget"), 1)
            dve.wait_ge(G("forget"), 4)
            for h in range(4):
                TS(KE[h], KD[h], -1.0, 1.0, MUL, ADD)
            for h in range(4):
                dve.wait_ge(G("log_f"), h + 1)
                link(v.tensor_tensor_scan(CAT2[4 + h], C("hreset"), CAT2[h], 0.0, MUL, ADD))
                b3 = CAT2[4 + h].rearrange("p (n c) -> p n c", c=HC)
                TT(KD[h].rearrange("p (n c) -> p n c", c=HC), b3[:, :, HC - 1:HC].to_broadcast([P, S // HC, HC]), b3,
                   SUB).then_inc(G("scanned"), 1)

            def gates(h):
                dve.wait_ge(G("exp_b"), h + 1)
                freed(dve, ("qr", h))
                TT(QE[h], QE[h], CAT2[h], MUL)
                link(TT(KD[h], KE[h], KD[h], MUL))
                link(TT(KE[h], KE[h], CAT2[4 + h], MUL))
                TS(sm[:, 120:121], sm[:, 32:33], 1.0, None, MUL).then_inc(G("g_ready"), 1)

            def a_max(u):
                h, qt = A2[u]
                w = P * (qt + 1)
                o = 8 + 4 * (u % 2)
                bk = full(dve, ("as", u))
                if u >= 2:
                    full(dve, ("apt", u - 2))
                release(STT(tmp[:, u % 2, 0:w], bk[:, 0:w], 0.125, neg[qt][:, 0:w], MUL, ADD), ("as", u))
                freed(dve, ("as", u))
                link(v.tensor_reduce(sm[:, o:o + 1], tmp[:, u % 2, 0:w], AX.X, ALU.max))
                TS(sm[:, o + 1:o + 2], sm[:, o:o + 1], -1.0, None, MUL).then_inc(G("a_max"), 1)

            def a_p(u):
                h, qt = A2[u]
                w = P * (qt + 1)
                o = 8 + 4 * (u % 2)
                e = tmp[:, u % 2, 0:w]
                dve.wait_ge(G("a_exp"), u + 1)
                link(v.tensor_tensor_reduce(out=e, in0=e, in1=cnt[qt][:, 0:w], scale=1.0, scalar=0.0, op0=MUL,
                                            op1=ADD, accum_out=sm[:, o + 2:o + 3]))
                link(v.reciprocal(sm[:, o + 3:o + 4], sm[:, o + 2:o + 3]))
                TS(e, e, sm[:, o + 3:o + 4], None, MUL).then_inc(G("a_p"), 1)

            for u in range(len(A2) + 1):
                if u < len(A2):
                    a_max(u)
                if u >= 1:
                    a_p(u - 1)
                if u in (2, 5, 8, 11):
                    gates(u // 3)
            link(v.memset(AM, 0.0))
            for h in range(4):
                bk = full(dve, ("am", h))
                if h:
                    full(dve, ("or", h - 1))
                for tt in range(2):
                    ins = v.copy_predicated(AM[:, P * tt:P * tt + P], C("hmask").bitcast(I32), bk[:, P * tt:P * tt + P])
                release(ins, ("am", h))
                for n in range(7):
                    bk = full(dve, ("dl", h, n % 4))
                    d = bk[:, P * (n // 4):P * (n // 4) + P]
                    if n == 0:
                        ins = v.tensor_copy(ST[:, 1, :], d)
                    else:
                        ins = STT(ST[:, n + 1, :], ST[:, n, :], DECAY(h)[:, n:n + 1], d, MUL, ADD)
                    if n >= 3:
                        release(ins, ("dl", h, n % 4))
                        freed(dve, ("dl", h, n % 4))
                    else:
                        link(ins)
                TS(sm[:, 121:122], sm[:, 32:33], 1.0, None, MUL).then_inc(G("states"), 1)
            for c in range(4):
                dve.wait_ge(G("as_rstd"), c + 1)
                STT(CAT2[c], OA[c], V1("anw", c), tmp[:, 4 + c // 2, S * (c % 2):S * (c % 2) + S], MUL,
                    MUL).then_inc(G("cat2"), 1)
            for h in range(4):
                dve.wait_ge(G("or_rstd"), h + 1)
                link(STT(OR[h], OR[h], V1("hnw", h), tmp[:, h // 2, S * (h % 2):S * (h % 2) + S], MUL, MUL))
                freed(dve, ("grg", h))
                TT(CAT2[4 + h], OR[h], GR[h], MUL).then_inc(G("cat2"), 1)

            def post(gain, part, rs, ys, sig):
                for c in range(DC):
                    link(STT(ys[c], ys[c], V1(gain, c), rs, MUL, MUL))
                    STT(xT[:, c, 0:S], ys[c], modv[:, 2, 8 * part + c, 0:1], xT[:, c, 0:S], MUL, ADD).then_inc(sig, 1)

            dve.wait_ge(G("post_rstd"), 1)
            post("gqm", 2, tmp[:, 0, 0:S], Y2, G("x_mixed"))
            norm(5)

            v.memset(big[:, 23, 0:P], 0.0).then_inc(G("zeroed"), 1)
            top = sm[:, 40:56]
            idxf = sm[:, 56:64]
            for tt in range(2):
                bk = full(dve, ("lg", tt))
                release(v.tensor_copy(lg[:, tt, :], bk[:, 0:NE]), ("lg", tt))
                freed(dve, ("lg", tt))
                link(v.max(top[:, 8 * tt:8 * tt + 8], lg[:, tt, :]))
                v.max_index(topi[:, 0:8], top[:, 8 * tt:8 * tt + 8], lg[:, tt, :])
                link(TS(sm[:, 104 + tt:105 + tt], top[:, 8 * tt:8 * tt + 1], -1.0, None, MUL))
                link(v.tensor_copy(idxf, topi[:, 0:8]))
                link(TS(msk[:, tt, :], C("iota", 0, NE), idxf[:, 0:1], None, ALU.is_equal))
                for i in range(1, 4):
                    ins = STT(msk[:, tt, :], C("iota", 0, NE), idxf[:, i:i + 1], msk[:, tt, :], ALU.is_equal, ADD)
                    if i < 3:
                        link(ins)
                ins.then_inc(G("mask"), 1)
                dve.wait_ge(G("mask"), tt + 1)
                TS(sm[:, 122:123], sm[:, 32:33], 1.0, None, MUL).then_inc(G("neg_top"), 1)
            for tt in range(2):
                dve.wait_ge(G("gate_exp"), tt + 1)
                link(v.tensor_tensor_reduce(out=gate[:, tt, :], in0=rt[:, 32 * tt:32 * tt + 32], in1=msk[:, tt, :],
                                            scale=1.0, scalar=0.0, op0=MUL, op1=ADD,
                                            accum_out=sm[:, 106 + tt:107 + tt]))
                link(v.reciprocal(sm[:, 108 + tt:109 + tt], sm[:, 106 + tt:107 + tt]))
                link(TS(gate[:, tt, :], gate[:, tt, :], sm[:, 108 + tt:109 + tt], None, MUL))
                bk = full(dve, ("rank", tt))
                release(STT(posn[:, tt, :], bk[:, 0:NE], 1000.0, msk[:, tt, :], ADD, MUL), ("rank", tt))
                freed(dve, ("rank", tt))
                link(TS(posn[:, tt, :], posn[:, tt, :], -1000.0, None, ADD))
            nb = lr[:, 0, :]
            bk = full(dve, "count")
            link(TS(nb, bk[:, 0:NE], float(CAP), None, ALU.is_gt))
            for i in range(2, 4):
                ins = STT(nb, bk[:, 0:NE], float(CAP * i), nb, ALU.is_gt, ADD)
                if i == 2:
                    link(ins)
            release(ins, "count")
            freed(dve, "count")
            link(TS(nb, nb, 1.0, None, ADD))
            link(v.tensor_tensor_scan(cum, C("ones", 0, NE), nb, 0.0, MUL, ADD))
            cb = cum.unsqueeze(1).to_broadcast([P, MAXB + 1, NE])
            link(TT(le, cb, C("bidx").unsqueeze(2).to_broadcast([P, MAXB + 1, NE]), ALU.is_le))
            link(v.tensor_reduce(le3, le, AX.X, ADD))
            link(TS(le3, le3, float(NE - 1), None, ALU.min))
            v.tensor_copy(itab[:, 0, :], le3)
            TS(itab[:, 1, 0:NE], cum, -1.0, None, ADD)
            link(v.tensor_copy(itab[:, 2, MAXB:MAXB + 1], cum[:, NE - 1:NE]))
            TS(sm[:, 123:124], sm[:, 32:33], 1.0, None, MUL).then_inc(G("tables"), 1)
            link(TT(le2, le, cb, MUL))
            link(v.tensor_reduce(offt, le2, AX.X, ALU.max))
            link(TT(offt, C("bidx"), offt, SUB))
            link(TS(offt, offt, float(CAP), None, MUL))
            TS(sm[:, 124:125], sm[:, 32:33], 1.0, None, MUL).then_inc(G("tables"), 1)

            t4, t5, t6, t7 = MOE["turns"][4:8]

            def select(e, b, before):
                if before is not None:
                    dve.wait_ge(bank_full[6], before)
                for tt in range(2):
                    ins = TS(SEL[:, tt, :], C("iota"), offt[:, bass.ds(b, 1)], posn[:, tt, bass.ds(e, 1)], ADD,
                             ALU.is_equal)
                ins.then_inc(G("sel"), 1)

            def gselect(e, b, done, before, ready):
                if before is not None:
                    dve.wait_ge(bank_full[6], before)
                for tt in range(2):
                    ins = TS(SGS[:, tt, :], C("iota"), offt[:, bass.ds(b, 1)], posn[:, tt, bass.ds(e, 1)], ADD,
                             ALU.is_equal)
                ins.then_inc(G("gsel_raw"), 1)
                dve.wait_ge(G("gsel_raw"), done)
                for tt in range(2):
                    ins = TS(SGS[:, tt, :], SGS[:, tt, :], gate[:, tt, bass.ds(e, 1)], None, MUL)
                ins.then_inc(ready, 1)

            g3 = GL.rearrange("p (j s) -> p j s", s=CAP)
            l3 = LI.rearrange("p (j s) -> p j s", s=CAP)

            def activate(e, f4, f5, b5):
                dve.wait_ge(bank_full[4], f4)
                TT(g3, bank[4][:, :].rearrange("p (j s) -> p j s", s=CAP),
                   V("bgu")[:, bass.ds(e * 16, 8)].unsqueeze(2).to_broadcast([P, 8, CAP]), ADD).then_inc(bank_free[4], 1)
                dve.wait_ge(bank_free[4], f4)
                TS(GL, GL, 7.0, None, ALU.min).then_inc(G("glu_in"), 1)
                dve.wait_ge(bank_full[5], f5)
                TT(l3, bank[5][:, :].rearrange("p (j s) -> p j s", s=CAP),
                   V("bgu")[:, bass.ds(e * 16 + 8, 8)].unsqueeze(2).to_broadcast([P, 8, CAP]), ADD).then_inc(bank_free[5], 1)
                dve.wait_ge(bank_free[5], f5)
                TS(LI, LI, 7.0, -7.0, ALU.min, ALU.max).then_inc(G("lin"), 1)
                dve.wait_ge(G("lin"), b5 * 2 + 1)
                STT(LI, LI, 1.0, GL, ADD, MUL).then_inc(G("lin"), 1)
                dve.wait_ge(G("lin"), b5 * 2 + 2)
                dve.wait_ge(G("glu_sig"), b5 + 1)
                TT(AC, l3, SI.rearrange("p (j s) -> p j s", s=CAP), MUL).then_inc(G("moe_act"), 1)

            def take_down(e, n7):
                dve.wait_ge(bank_full[7], n7)
                TT(YT, bank[7][:, :].rearrange("p (j s) -> p j s", s=CAP),
                   V("bdn")[:, bass.ds(e * 8, 8)].unsqueeze(2).to_broadcast([P, 8, CAP]), ADD).then_inc(bank_free[7], 1)

            def take_y(n7):
                dve.wait_ge(bank_full[7], n7)
                v.tensor_copy(YK[:, 1, :], bank[7][0:CAP, :]).then_inc(bank_free[7], 1)

            dve.wait_ge(G("tables"), 2)
            nblk = dve.value_load(itab[0:1, 2, MAXB:MAXB + 1], min_val=NE, max_val=MAXB - 1)
            select(0, 0, None)
            e1 = dve.value_load(itab[0:1, 0, 1:2], min_val=0, max_val=NE - 1)
            select(e1, 1, t6 + 1)
            activate(0, t4 + 1, t5 + 1, 0)
            take_down(0, t7 + 1)
            with dve.Fori(1, nblk) as b:
                ep = dve.value_load(itab[0:1, 0, bass.ds(b - 1, 1)], min_val=0, max_val=NE - 1)
                e = dve.value_load(itab[0:1, 0, bass.ds(b, 1)], min_val=0, max_val=NE - 1)
                en = dve.value_load(itab[0:1, 0, bass.ds(b + 1, 1)], min_val=0, max_val=NE - 1)
                take_y(b * 2 + t7)
                gselect(ep, b - 1, b, b * 3 + (t6 - 2), G("gsel"))
                select(en, b + 1, b * 3 + (t6 - 1))
                activate(e, b + (t4 + 1), b + (t5 + 1), b)
                take_down(e, b * 2 + (t7 + 1))
            el = dve.value_load(itab[0:1, 0, bass.ds(nblk - 1, 1)], min_val=0, max_val=NE - 1)
            TS(sm[:, 125:126], sm[:, 32:33], 1.0, None, MUL).then_inc(G("loop_end"), 1)
            take_y(nblk * 2 + t7)
            gselect(el, nblk - 1, nblk, nblk * 3 + (t6 - 2), G("gsel_last"))

            dve.wait_ge(G("fin_rstd"), 1)
            post("gqf", 5, tmp[:, 0, 0:S], YF, G("x_final"))

        @block.sync
        def _(sp):
            sp.dma_start(xT[:, :, :], xin).then_inc(G("x_loaded"), 16)
            n0 = MOE["slot0"]

            def load(n, src, w):
                sp.dma_start(wring[:, n % RING, 0:w] if len(src.shape) == 2 else
                             wring[:, n % RING, 0:w].rearrange("p (k n) -> p k n", k=src.shape[1]),
                             src).then_inc(w_full[n % RING], 16)

            for n, (src, w) in enumerate(stream):
                if n >= RING:
                    sp.wait_ge(w_used, n - RING + 1)
                load(n, src, w)

            def expert(s, e):
                if s < GUC:
                    return w_gu[0, e].rearrange("(p k) n -> p k n", k=DC)[:, s, :]
                return w_down[0, e, 256 * (s - GUC):256 * (s - GUC) + 256, :].rearrange("(j p) n -> p j n", p=P)

            for s in range(RING):
                sp.wait_ge(w_used, n0 + s - RING + 1)
                load(n0 + s, expert(s, 0), SLOT)
            sp.wait_ge(G("tables"), 1)
            with sp.Fori(1, NE) as e:
                c = sp.value_load(itab[0:1, 1, bass.ds(e - 1, 1)], min_val=0, max_val=MAXB - 2)
                for s in range(RING):
                    sp.wait_ge(G("moe_used"), c * RING + (s + 1))
                    src = (w_gu[0, bass.ds(e, 1)].rearrange("a (p k) n -> p k (a n)", k=DC)[:, s, :] if s < GUC else
                           w_down[0, bass.ds(e, 1), 256 * (s - GUC):256 * (s - GUC) + 256, :].rearrange(
                               "a (j p) n -> p j (a n)", p=P))
                    load(n0 + s, src, SLOT)
            for c in range(DC):
                sp.wait_ge(G("x_final"), c + 1)
                sp.dma_start(out[P * c:P * c + P, :], xT[:, c, 0:S]).then_inc(G("stored"), 16)
            sp.wait_ge(G("stored"), 16 * DC)


def columns(a):
    return np.asarray(a).reshape(-1, P).T


def kernel(**inputs):
    import concourse.bacc as _bacc
    from concourse.bass_utils import run_bass_kernel_spmd as _run

    i = {k: np.asarray(a) for k, a in inputs.items()}
    packed = {
        "cin": np.stack([i["c"][0].reshape(P, 8), i["c_ctx"].reshape(P, 8)], axis=2).reshape(P, 16),
        "c2": i["c_2"][0].reshape(P, 8),
        "mod_b0": columns(i["mod_b"][0]), "mod_b1": columns(i["mod_b"][1]), "mod_b2": columns(i["b_ada_2"][0]),
        "n1_0": columns(i["norm1_g"][0]), "n2_0": columns(i["norm2_g"][0]),
        "n1_1": columns(i["norm1_g"][1]), "n2_1": columns(i["norm2_g"][1]),
        "scw": columns(i["sc_conv_w"][0]),
        "qg": np.tile(i["da_q_norm"][0], 2)[:, None], "kg": np.tile(i["da_k_norm"][0], 2)[:, None],
        "lq1": np.tile(i["da_lq1"][0], 2)[:, None], "lk1": np.tile(i["da_lk1"][0], 2)[:, None],
        "lq2": np.tile(i["da_lq2"][0], 2)[:, None], "lk2": np.tile(i["da_lk2"][0], 2)[:, None],
        "subln": columns(i["da_subln_g"][0]), "pscale": columns(i["pool_scale"][0]),
        "decf": np.tile(i["ret_decay_f"], (P, 1)), "decb": np.tile(i["ret_decay_b"], (P, 1)),
        "gng": columns(i["ret_gn_g"][0]),
        "fcw_0": columns(i["ffn_conv_w"][0]), "fcw_1": columns(i["ffn_conv_w"][1]),
        "fcb_0": columns(i["ffn_conv_b"][0]), "fcb_1": columns(i["ffn_conv_b"][1]),
        "gpm": columns(i["g_pre_mix_2"]), "gqm": columns(i["g_post_mix_2"]), "anw": columns(i["attn_norm_w_2"]),
        "hlb": columns(i["hgrn_lb_2"]), "hnw": columns(i["hgrn_norm_w_2"]),
        "gpf": columns(i["g_pre_ffn_2"]), "gqf": columns(i["g_post_ffn_2"]),
        "bgu": columns(i["b_gu_2"]), "bdn": columns(i["b_down_2"]),
    }
    vec = np.concatenate([packed[n].reshape(P, w) for n, w in VEC], axis=1)
    tab, late = tables()
    x = np.concatenate([i["x"][0], i["ctx"][0]], axis=0)
    xin = x.T.reshape(DC, P, T2).transpose(1, 0, 2)
    arrays = {"xin": xin, "vec": vec, "tab": tab, "late": late, "brouter": i["b_router_2"]}
    for n in ("mod_w", "ev_w_in", "ev_w_out", "od_w_in", "od_w_out", "pool_w", "ffn_w_up", "ffn_w_down", "w_ada_2",
              "w_in_2", "w_out_2", "w_router_2", "w_gu_2", "w_down_2"):
        arrays[n] = i[n]
    arrays = {n: np.ascontiguousarray(a) for n, a in arrays.items()}
    nc = _bacc.Bacc("TRN2", target_bir_lowering=False, num_devices=1)
    args = [nc.dram_tensor("in_" + n, a.shape, mybir.dt.from_np(a.dtype), kind="ExternalInput").ap()
            for n, a in arrays.items()]
    args.append(nc.dram_tensor("out_x", (D, S), F32, kind="ExternalOutput").ap())
    program(nc, *args)
    r = _run(nc, [{"in_" + n: a for n, a in arrays.items()}], core_ids=[0])
    return r.results[0]["out_x"].T.reshape(1, S, D)
```
